# Optimizing a Trainium2 kernel written in Bass

```python
import jax, jax.numpy as jnp
from jax import lax
import numpy as np

D_MODEL = 1024
BATCH = 1
SEQ = 256
DEPTH = 2

EPS = 1e-6
ROPE_THETA = 10000.0
BLOCK = 128
MLA_HEADS = 4
MLA_Q_RANK = 256
MLA_KV_RANK = 128
MLA_NOPE = 128
MLA_ROPE = 64
MLA_V = 128
MLA_QK = MLA_NOPE + MLA_ROPE
MLA_WIDTH = MLA_HEADS * MLA_V
SWA_HEADS = 8
SWA_KV_HEADS = 2
SWA_HEAD_DIM = 64
WINDOW = 128
SWA_WIDTH = SWA_HEADS * SWA_HEAD_DIM
MIX_WIDTH = MLA_WIDTH + SWA_WIDTH
IN_SPLITS = (MLA_Q_RANK, MLA_KV_RANK, MLA_ROPE,
             SWA_HEADS * SWA_HEAD_DIM, SWA_KV_HEADS * SWA_HEAD_DIM, SWA_KV_HEADS * SWA_HEAD_DIM)
IN_COLS = sum(IN_SPLITS)
D_FF = 2816

kernel_name = "hybrid_mla_swa_sink_macaron"

def rmsnorm(t, g):
    tf = t.astype(jnp.float32)
    out = tf * lax.rsqrt(jnp.mean(tf * tf, axis=-1, keepdims=True) + EPS)
    return (out * g.astype(jnp.float32)).astype(t.dtype)

def swiglu(t, w_gate, w_up, w_down):
    return (jax.nn.silu(t @ w_gate) * (t @ w_up)) @ w_down

def rope_table(seq, dim):
    pos = jnp.arange(seq, dtype=jnp.float32)
    inv = 1.0 / (ROPE_THETA ** (jnp.arange(0, dim, 2, dtype=jnp.float32) / dim))
    ang = pos[:, None] * inv[None, :]
    return jnp.cos(ang), jnp.sin(ang)

def apply_rope(t, cos, sin):
    half = t.shape[-1] // 2
    t1 = t[..., :half].astype(jnp.float32)
    t2 = t[..., half:].astype(jnp.float32)
    c = cos[None, :, None, :]
    s = sin[None, :, None, :]
    return jnp.concatenate([t1 * c - t2 * s, t2 * c + t1 * s], axis=-1).astype(t.dtype)

def dense_causal_attention(q, k, v, scale):
    B, S, H, Dq = q.shape
    nb = S // BLOCK
    qb = q.reshape(B, nb, BLOCK, H, Dq).transpose(1, 0, 2, 3, 4)
    k_pos = jnp.arange(S)

    def one_block(args):
        q_blk, i = args
        s = jnp.einsum('bqhd,bkhd->bhqk', q_blk, k, preferred_element_type=jnp.float32) * scale
        q_pos = i * BLOCK + jnp.arange(BLOCK)
        mask = k_pos[None, :] <= q_pos[:, None]
        s = jnp.where(mask[None, None], s, -jnp.inf)
        p = jax.nn.softmax(s, axis=-1)
        return jnp.einsum('bhqk,bkhd->bqhd', p.astype(v.dtype), v)

    out = lax.map(one_block, (qb, jnp.arange(nb)))
    return out.transpose(1, 0, 2, 3, 4).reshape(B, S, H, v.shape[-1])

def sliding_window_sink_attention(q, k, v, sinks, scale):
    B, S, H, D = q.shape
    KV = k.shape[2]
    G = H // KV
    nb = S // BLOCK
    qb = q.reshape(B, nb, BLOCK, KV, G, D)

    def band(t):
        tb = t.reshape(B, nb, BLOCK, KV, D)
        prev = jnp.pad(tb[:, :-1], ((0, 0), (1, 0), (0, 0), (0, 0), (0, 0)))
        return jnp.concatenate([prev, tb], axis=2)

    kb, vb = band(k), band(v)
    s = jnp.einsum('bnqcgd,bnkcd->bncgqk', qb, kb, preferred_element_type=jnp.float32) * scale
    q_rel = jnp.arange(BLOCK)[:, None] + BLOCK
    k_rel = jnp.arange(2 * BLOCK)[None, :]
    dist = q_rel - k_rel
    in_window = (dist >= 0) & (dist < WINDOW)
    k_abs = jnp.arange(nb)[:, None, None] * BLOCK + k_rel[None] - BLOCK
    valid = in_window[None] & (k_abs >= 0)
    s = jnp.where(valid[None, :, None, None], s, -jnp.inf)
    sink = sinks.astype(jnp.float32).reshape(KV, G)[None, None, :, :, None, None]
    m = jnp.maximum(jnp.max(s, axis=-1, keepdims=True), sink)
    e = jnp.exp(s - m)
    p = e / (jnp.sum(e, axis=-1, keepdims=True) + jnp.exp(sink - m))
    out = jnp.einsum('bncgqk,bnkcd->bnqcgd', p.astype(v.dtype), vb)
    return out.reshape(B, S, H, D)

def setup_inputs(seed: int = 0) -> dict:
    key = jax.random.key(seed)
    ks = iter(jax.random.split(key, 32))

    def w(shape, fan_in):
        return jax.random.normal(next(ks), shape, jnp.float32) * (fan_in ** -0.5)

    def gain(shape):
        return 1.0 + 0.02 * jax.random.normal(next(ks), shape, jnp.float32)

    L = DEPTH
    return {
        "x": jax.random.normal(next(ks), (BATCH, SEQ, D_MODEL), jnp.float32),
        "ffn1_norm": gain((L, D_MODEL)),
        "ffn1_w_gate": w((L, D_MODEL, D_FF), D_MODEL),
        "ffn1_w_up": w((L, D_MODEL, D_FF), D_MODEL),
        "ffn1_w_down": w((L, D_FF, D_MODEL), D_FF),
        "mix_norm": gain((L, D_MODEL)),
        "w_in": w((L, D_MODEL, IN_COLS), D_MODEL),
        "mla_q_a_norm": gain((L, MLA_Q_RANK)),
        "mla_w_q_b": w((L, MLA_Q_RANK, MLA_HEADS * MLA_QK), MLA_Q_RANK),
        "mla_kv_a_norm": gain((L, MLA_KV_RANK)),
        "mla_w_kv_b": w((L, MLA_KV_RANK, MLA_HEADS * (MLA_NOPE + MLA_V)), MLA_KV_RANK),
        "mla_q_norm": gain((L, MLA_QK)),
        "mla_k_norm": gain((L, MLA_QK)),
        "swa_q_norm": gain((L, SWA_HEAD_DIM)),
        "swa_k_norm": gain((L, SWA_HEAD_DIM)),
        "swa_sinks": 0.5 * jax.random.normal(next(ks), (L, SWA_HEADS), jnp.float32),
        "mla_out_norm": gain((L, MLA_WIDTH)),
        "swa_out_norm": gain((L, SWA_WIDTH)),
        "w_o": w((L, MIX_WIDTH, D_MODEL), MIX_WIDTH),
        "ffn2_norm": gain((L, D_MODEL)),
        "ffn2_w_gate": w((L, D_MODEL, D_FF), D_MODEL),
        "ffn2_w_up": w((L, D_MODEL, D_FF), D_MODEL),
        "ffn2_w_down": w((L, D_FF, D_MODEL), D_FF),
    }

def reference(x, ffn1_norm, ffn1_w_gate, ffn1_w_up, ffn1_w_down, mix_norm, w_in,
              mla_q_a_norm, mla_w_q_b, mla_kv_a_norm, mla_w_kv_b, mla_q_norm, mla_k_norm,
              swa_q_norm, swa_k_norm, swa_sinks, mla_out_norm, swa_out_norm, w_o,
              ffn2_norm, ffn2_w_gate, ffn2_w_up, ffn2_w_down):
    B, S, _ = x.shape
    cos, sin = rope_table(S, MLA_ROPE)
    split_idx = np.cumsum(IN_SPLITS)[:-1].tolist()
    mla_scale = MLA_QK ** -0.5
    swa_scale = SWA_HEAD_DIM ** -0.5

    for l in range(DEPTH):
        x = x + 0.5 * swiglu(rmsnorm(x, ffn1_norm[l]), ffn1_w_gate[l], ffn1_w_up[l], ffn1_w_down[l])

        h = rmsnorm(x, mix_norm[l])
        c_q, c_kv, k_pe, q_s, k_s, v_s = jnp.split(h @ w_in[l], split_idx, axis=-1)

        q_a = (rmsnorm(c_q, mla_q_a_norm[l]) @ mla_w_q_b[l]).reshape(B, S, MLA_HEADS, MLA_QK)
        kv_a = (rmsnorm(c_kv, mla_kv_a_norm[l]) @ mla_w_kv_b[l]).reshape(B, S, MLA_HEADS, MLA_NOPE + MLA_V)
        k_nope, v_a = kv_a[..., :MLA_NOPE], kv_a[..., MLA_NOPE:]
        k_a = jnp.concatenate(
            [k_nope, jnp.broadcast_to(k_pe[:, :, None, :], (B, S, MLA_HEADS, MLA_ROPE))], axis=-1)
        q_a = rmsnorm(q_a, mla_q_norm[l])
        k_a = rmsnorm(k_a, mla_k_norm[l])
        q_a = jnp.concatenate([q_a[..., :MLA_NOPE], apply_rope(q_a[..., MLA_NOPE:], cos, sin)], axis=-1)
        k_a = jnp.concatenate([k_a[..., :MLA_NOPE], apply_rope(k_a[..., MLA_NOPE:], cos, sin)], axis=-1)
        out_a = dense_causal_attention(q_a, k_a, v_a, mla_scale).reshape(B, S, MLA_WIDTH)

        q_b = rmsnorm(q_s.reshape(B, S, SWA_HEADS, SWA_HEAD_DIM), swa_q_norm[l])
        k_b = rmsnorm(k_s.reshape(B, S, SWA_KV_HEADS, SWA_HEAD_DIM), swa_k_norm[l])
        v_b = v_s.reshape(B, S, SWA_KV_HEADS, SWA_HEAD_DIM)
        q_b = apply_rope(q_b, cos, sin)
        k_b = apply_rope(k_b, cos, sin)
        out_b = sliding_window_sink_attention(q_b, k_b, v_b, swa_sinks[l], swa_scale).reshape(B, S, SWA_WIDTH)

        mixed = jnp.concatenate([rmsnorm(out_a, mla_out_norm[l]), rmsnorm(out_b, swa_out_norm[l])], axis=-1)
        x = x + mixed @ w_o[l]

        x = x + 0.5 * swiglu(rmsnorm(x, ffn2_norm[l]), ffn2_w_gate[l], ffn2_w_up[l], ffn2_w_down[l])
    return x


_drawn_inputs = setup_inputs


def setup_inputs(seed=0):
    import zlib

    import numpy as np

    out = dict(_drawn_inputs(seed))
    spreads = {}
    factors = {'ffn1_norm': 4.358,
     'mla_q_a_norm': 6.119,
     'mla_kv_a_norm': 3.104,
     'mla_q_norm': 6.181,
     'mla_k_norm': 6.209,
     'swa_q_norm': 6.41,
     'swa_k_norm': 6.016,
     'swa_sinks': 30.481,
     'mla_out_norm': 11.49,
     'swa_out_norm': 11.419,
     'ffn2_norm': 7.879}
    for name, (base, spread) in spreads.items():
        noise = np.random.default_rng([zlib.crc32(name.encode()), seed]).standard_normal(out[name].shape)
        drawn = base * np.exp(spread * noise) if base else spread * noise
        out[name] = __import__('jax').numpy.asarray(drawn.astype(out[name].dtype))
    for name, factor in factors.items():
        out[name] = (out[name] * factor).astype(out[name].dtype)
    return out
```

```python
from contextlib import ExitStack

import concourse.bass as bass
from concourse import mybir

ALU = mybir.AluOpType
ACT = mybir.ActivationFunctionType
AX_X = mybir.AxisListType.X
F32 = mybir.dt.float32
F32R = mybir.dt.float32r
BF16 = mybir.dt.bfloat16

P = 128
D = 1024
SEQ = 256
DEPTH = 2
TB = SEQ // P
KD = D // P
EPS = 1e-6
FF = 2816
GC = 256
NG = FF // GC
QR, KVR = 256, 128
MH, NOPE, ROPE, MV = 4, 128, 64, 128
SH, SKV, SD = 8, 2, 64
MLA_QK = NOPE + ROPE
MLA_SCALE = MLA_QK ** -0.5
SWA_SCALE = SD ** -0.5
MASKED = -1e30

RAW = 4
UNITS = 6
HC = 1024
FFN_UNITS = 3 * NG
MIX_UNITS = 10
LU = 2 * FFN_UNITS + MIX_UNITS
FFN_AT = (0, FFN_UNITS + MIX_UNITS)
MIX_AT = FFN_UNITS
NORMS = 4

SG_QA, SG_KVA = 0, QR
SG_SQ = QR + KVR
SG_SK, SG_MQ, SG_MK, SG_SINK = SG_SQ + 64, SG_SQ + 128, SG_SQ + 192, SG_SQ + 256
SG = SG_SINK + SH

CQN, CQR, CKR, CKN, CSQ, CSK, CHUNKS = 0, 4, 6, 8, 12, 16, 17


def up_unit(g):
    return 2 * g if g < 2 else 3 * g - 1


def down_unit(g):
    return 4 + 3 * g if g < NG - 1 else FFN_UNITS - 1


def unit_slots():
    ffn = [None] * FFN_UNITS
    for g in range(NG):
        ffn[up_unit(g)], ffn[up_unit(g) + 1] = 3 * (g % 2), 3 * (g % 2) + 1
        ffn[down_unit(g)] = 3 * (g % 2) + 2
    slots = ffn + [3, 4, 5, 0, 1, 2, 3, 4, 5, 2] + ffn
    twice = slots + slots
    back = []
    for u in range(LU, 2 * LU):
        last = max(v for v in range(u) if twice[v] == twice[u])
        back.append(min(u - last, UNITS))
    return slots, back


SLOT, BACK = unit_slots()


def hybrid_trunk(nc, x_in, stream, norm_gains, small_gains, col_gains, rope, out):
    with ExitStack() as ctx:
        def sb(name, shape, dt=F32):
            return ctx.enter_context(nc.sbuf_tensor(name, shape, dt))

        def pb(name, shape):
            return ctx.enter_context(nc.psum_tensor(name, shape, F32))

        def sem(name):
            return ctx.enter_context(nc.semaphore(name))

        def heads(ap, n):
            return ap.rearrange("p (n d) -> p n d", n=n)

        raw = sb("raw", [P, RAW, HC])
        whi = sb("whi", [P, UNITS, 2 * HC], F32R)
        wlo = sb("wlo", [P, UNITS, 2 * HC], F32R)
        x = sb("x", [P, TB, D])
        act_hi = sb("act_hi", [P, TB, KD, P], F32R)
        act_lo = sb("act_lo", [P, TB, KD, P], F32R)
        gain = sb("gain", [P, 2, D])
        sgain = sb("sgain", [P, SG])
        cgain = sb("cgain", [P, 2])
        cs = sb("cs", [P, TB, 2, ROPE])
        xn = sb("xn", [P, D])
        rot = sb("rot", [P, 2 * 640])
        rot_in, rot_tmp, attn = rot[:, 0:640], rot[:, 640:1280], rot[:, 0:D]
        ht_hi = sb("ht_hi", [P, TB, 2, P], F32R)
        ht_lo = sb("ht_lo", [P, TB, 2, P], F32R)
        work = sb("work", [P, 4, 512])
        silu = heads(work[:, 0, :], TB)
        h = heads(work[:, 1, :], TB)
        probs = work[:, 0:2, :]
        probs_t = work[:, 2:4, :]
        latent = sb("latent", [P, QR + KVR])
        swa_raw = sb("swa_raw", [P, 640])
        kpe = sb("kpe", [P, TB, ROPE])
        kpe_g = sb("kpe_g", [P, ROPE])
        qkn = sb("qkn", [P, CHUNKS, P])
        qt = sb("qt", [P, TB, 10, P])
        kt = sb("kt", [P, 7, TB, P])
        v_mla = sb("v_mla", [P, TB, MH * MV])
        v_swa = sb("v_swa", [P, TB, SKV * SD])
        ident = sb("ident", [P, P])
        ident_b = sb("ident_b", [P, P], BF16)
        masks = sb("masks", [P, 2, P], BF16)
        consts = sb("consts", [P, 2, 16])
        ss_x = sb("ss_x", [P, TB, 2])
        rs_x = sb("rs_x", [P, TB, 2])
        ss_c = sb("ss_c", [P, TB, 2])
        rs_c = sb("rs_c", [P, TB, 2])
        ss_s = sb("ss_s", [P, TB, 10])
        rs_s = sb("rs_s", [P, TB, 10])
        ss_part = sb("ss_part", [P, TB, 12])
        ss_pe = sb("ss_pe", [P, TB, 1])
        ss_m = sb("ss_m", [P, TB, 8])
        rs_m = sb("rs_m", [P, TB, 8])
        top = sb("top", [P, 2, 4])
        shift = sb("shift", [P, 2, 4])
        sink_gap = sb("sink_gap", [P, TB, SH])
        sink_e = sb("sink_e", [P, TB, SH])
        den = sb("den", [P, TB, MH + SH])
        rden = sb("rden", [P, TB, MH + SH])
        maxi = sb("maxi", [P, 2, 4])

        UV = [pb(f"UV{t}", [P, 2, 512]) for t in range(TB)]
        A = [pb(f"A{t}", [P, 2, 512]) for t in range(TB)]

        raw_landed = [sem(f"raw_landed{r}") for r in range(RAW)]
        hi_done = sem("hi_done")
        split_done = sem("split_done")
        unit_freed = sem("unit_freed")
        x_loaded = sem("x_loaded")
        rope_loaded = sem("rope_loaded")
        gain_loaded = [sem("gain_loaded0"), sem("gain_loaded1")]
        small_loaded = sem("small_loaded")
        const_ready = sem("const_ready")
        pool_step = sem("pool_step")
        x_ready = sem("x_ready")
        ss_ready = sem("ss_ready")
        rstd_ready = sem("rstd_ready")
        xn_ready = sem("xn_ready")
        xt_ready = sem("xt_ready")
        act_hi_done = sem("act_hi_done")
        act_ready = sem("act_ready")
        up_done = sem("up_done")
        silu_done = sem("silu_done")
        h_ready = sem("h_ready")
        ht_psum = sem("ht_psum")
        ht_hi_done = sem("ht_hi_done")
        ht_ready = sem("ht_ready")
        sum_ready = sem("sum_ready")
        proj_done = sem("proj_done")
        latent_ss = sem("latent_ss")
        latent_rstd = sem("latent_rstd")
        latent_ready = sem("latent_ready")
        latent_psum = sem("latent_psum")
        latent_hi_done = sem("latent_hi_done")
        latent_act = sem("latent_act")
        swa_copied = sem("swa_copied")
        swa_ss = sem("swa_ss")
        swa_rstd = sem("swa_rstd")
        swa_used = sem("swa_used")
        mla_done = sem("mla_done")
        mla_squares = sem("mla_squares")
        mla_ss = sem("mla_ss")
        mla_rstd = sem("mla_rstd")
        qkn_ready = sem("qkn_ready")
        qk_psum = sem("qk_psum")
        qk_act = sem("qk_act")
        qk_dve = sem("qk_dve")
        scores_done = sem("scores_done")
        shift_ready = sem("shift_ready")
        probs_ready = sem("probs_ready")
        pt_psum = sem("pt_psum")
        pt_ready = sem("pt_ready")
        pv_done = sem("pv_done")
        attn_ready = sem("attn_ready")
        stored = sem("stored")

        def whi_half(unit, half):
            return whi[:, SLOT[unit], half * HC:(half + 1) * HC]

        def wlo_half(unit, half):
            return wlo[:, SLOT[unit], half * HC:(half + 1) * HC]

        def spread(ap, n):
            return ap.unsqueeze(2).to_broadcast([P, ap.shape[1], n])

        def over_heads(ap, n):
            return ap.unsqueeze(1).to_broadcast([P, n, ap.shape[1]])

        def score_banks(t):
            per = 4 // (t + 1)
            return [(True, [0, 2]), (True, [1, 3])] + [(False, list(range(i, i + per))) for i in range(0, SH, per)]

        BANKS = [score_banks(t) for t in range(TB)]
        LB = len(BANKS[0]) + len(BANKS[1])

        def bank_no(l, t, b):
            return l * LB + (len(BANKS[0]) if t else 0) + b

        block = ctx.enter_context(nc.Block())

        @block.sync
        def _(sp):
            for t in range(TB):
                sp.dma_start(x[:, t, :], x_in[t * P:(t + 1) * P, :]).then_inc(x_loaded, 16)
            with sp.Fori(0, DEPTH * LU * 2 // RAW) as i:
                for r in range(RAW):
                    sp.wait_ge(split_done, i * RAW + (r + 1))
                    sp.dma_start(raw[:, r, :], stream[bass.ds(i * RAW + r, 1)].rearrange("a p n -> (a p) n")
                                 ).then_inc(raw_landed[r], 16)
            for t in range(TB):
                sp.wait_ge(x_ready, DEPTH * 6 + t + 1)
                sp.dma_start(out[t * P:(t + 1) * P, :], x[:, t, :]).then_inc(stored, 16)
            sp.wait_ge(stored, 16 * TB)

        @block.gpsimd
        def _(pool):
            pool.dma_start(cs[:], rope.rearrange("t p a d -> p t a d")).then_inc(rope_loaded, 16)
            pool.memset(consts[:, 1, :], EPS)
            pool.memset(consts[:, 0, :], -0.5).then_inc(unit_freed, UNITS - 1)
            pool.memset(ident[:], 0.0)
            pool.memset(ident_b[:], 0.0)
            pool.memset(masks[:], 0.0).then_inc(pool_step, 1)
            pool.wait_ge(pool_step, 1)
            for m in (ident, ident_b):
                pool.affine_select(out=m[:], in_=m[:], compare_op=ALU.not_equal, fill=1.0, base=0,
                                   pattern=[[-1, P]], channel_multiplier=1)
            pool.affine_select(out=masks[:, 0, :], in_=masks[:, 0, :], compare_op=ALU.is_gt, fill=MASKED,
                               base=0, pattern=[[1, P]], channel_multiplier=-1)
            pool.affine_select(out=masks[:, 1, :], in_=masks[:, 1, :], compare_op=ALU.is_ge, fill=MASKED,
                               base=0, pattern=[[-1, P]], channel_multiplier=1).then_inc(const_ready, 1)

            def load_gain(l, k):
                src = norm_gains[bass.ds(l * NORMS + k, 1), :].to_broadcast([P, D])
                pool.dma_start(gain[:, k % 2, :], src).then_inc(gain_loaded[k % 2], 16)

            def rstd(rs, ms, ready):
                pool.tensor_tensor(rs, ms, consts[:, 1, 0:ms.shape[1]], ALU.add)
                pool.drain()
                pool.tensor_tensor(rs, rs, consts[:, 0, 0:ms.shape[1]], ALU.pow).then_inc(ready, 1)

            def norm_rstd(l, k, t):
                pool.wait_ge(ss_ready, l * 8 + (2 * k + t + 1))
                w = 2 if k == 2 else 1
                rstd(rs_x[:, t, 0:w], ss_x[:, t, 0:w], rstd_ready)

            with pool.Fori(0, DEPTH) as l:
                load_gain(l, 0)
                pool.dma_start(sgain[:], small_gains[bass.ds(l, 1), :].to_broadcast([P, SG])
                               ).then_inc(small_loaded, 16)
                pool.dma_start(cgain[:], col_gains[bass.ds(l, 1)].rearrange("a p c -> (a p) c")
                               ).then_inc(small_loaded, 16)
                norm_rstd(l, 0, 0)
                load_gain(l, 1)
                norm_rstd(l, 0, 1)
                pool.wait_ge(xn_ready, l * 8 + 2)
                load_gain(l, 2)
                norm_rstd(l, 1, 0)
                norm_rstd(l, 1, 1)
                pool.wait_ge(xn_ready, l * 8 + 4)
                load_gain(l, 3)
                def latent(t):
                    pool.wait_ge(latent_ss, l * TB + (t + 1))
                    rstd(rs_c[:, t, :], ss_c[:, t, :], latent_rstd)

                def window(t):
                    pool.wait_ge(swa_ss, l * TB + (t + 1))
                    rstd(rs_s[:, t, :], ss_s[:, t, :], swa_rstd)

                def mla(t):
                    pool.wait_ge(mla_ss, l * TB + (t + 1))
                    rstd(rs_m[:, t, :], ss_m[:, t, :], mla_rstd)

                latent(0)
                window(0)
                latent(1)
                mla(0)
                window(1)
                mla(1)
                for k in (2, 3):
                    for t in range(TB):
                        norm_rstd(l, k, t)

        @block.scalar
        def _(act):
            def split(l, unit, i=0, di=0):
                for half in range(2):
                    n = 2 * unit + half
                    act.wait_ge(raw_landed[n % RAW], l * (16 * 2 * LU // RAW) + i * (16 * 2 * di // RAW)
                                + 16 * (n // RAW + 1))
                    if half == 0:
                        act.wait_ge(unit_freed, l * LU + i * di + (unit - BACK[unit] + 1 + UNITS))
                    act.activation(whi_half(unit, half), raw[:, n % RAW, :], ACT.Copy).then_inc(hi_done, 1)

            def norm_squares(l, k, t):
                if k == 2:
                    act.wait_ge(attn_ready, l * 4 + (2 * t + 2))
                    for seg in range(2):
                        sq = act.activation(UV[t][:, seg, :], attn[:, seg * 512:(seg + 1) * 512], ACT.Square,
                                            scale=(D // 2) ** -0.5, accum_out=ss_x[:, t, seg:seg + 1])
                else:
                    act.wait_ge(x_ready, l * 6 + (2 * {0: 0, 1: 1, 3: 2}[k] + t + 1))
                    sq = act.activation(UV[t][:].rearrange("p a b -> p (a b)"), x[:, t, :], ACT.Square,
                                        scale=D ** -0.5, accum_out=ss_x[:, t, 0:1])
                sq.then_inc(ss_ready, 1)

            def norm_hi(l, k, t):
                for b in range(2):
                    act.wait_ge(xt_ready, l * 16 + (4 * k + 2 * t + b + 1))
                    act.activation(act_hi[:, t, 4 * b:4 * b + 4, :], UV[t][:, b, :], ACT.Copy
                                   ).then_inc(act_hi_done, 1)

            def ffn_group(l, f, g, i=0):
                n = l * (4 * NG) + i * 2 + (2 * (NG * f + g) + 1)

                def silu_block(t):
                    act.wait_ge(up_done, n + t)
                    act.activation(silu[:, t, :], UV[t][:, 0, 0:GC], ACT.Silu).then_inc(silu_done, 1)

                def ht_high(t):
                    act.wait_ge(ht_psum, n + t)
                    act.activation(ht_hi[:, t], UV[t][:, 1, 0:GC], ACT.Copy).then_inc(ht_hi_done, 1)

                silu_block(0)
                split(l, FFN_AT[f] + down_unit(g), i, 3)
                if g == NG - 1 and f == 0:
                    split(l, MIX_AT + 0)
                    split(l, MIX_AT + 1)
                silu_block(1)
                ht_high(0)
                if g + 2 < NG:
                    split(l, FFN_AT[f] + up_unit(g + 2), i, 3)
                    split(l, FFN_AT[f] + up_unit(g + 2) + 1, i, 3)
                ht_high(1)

            def ffn(l, f):
                k = 3 * f
                for t in range(TB):
                    norm_squares(l, k, t)
                    norm_hi(l, k, t)
                split(l, FFN_AT[f] + 2)
                split(l, FFN_AT[f] + 3)
                ffn_group(l, f, 0)
                with act.Fori(0, NG - 3, 2) as i:
                    ffn_group(l, f, 1, i)
                    ffn_group(l, f, 2, i)
                ffn_group(l, f, NG - 2)
                ffn_group(l, f, NG - 1)

            def latent_and_window(l, t):
                act.wait_ge(proj_done, l * TB + (t + 1))
                if t == 1:
                    act.wait_ge(latent_ready, l * TB + t)
                    act.wait_ge(swa_used, l * TB + t)
                act.activation(latent[:], A[t][:, 0, 0:QR + KVR], ACT.Copy)
                act.activation(swa_raw[:, 512:640], A[t][:, 0, QR + KVR:512], ACT.Copy)
                act.activation(swa_raw[:, 0:512], A[t][:, 1, :], ACT.Copy)
                act.activation(v_swa[:, t, :], UV[t][:, 0, 0:128], ACT.Copy)
                act.activation(kpe[:, t, :], UV[t][:, 0, 128:192], ACT.Copy)
                act.drain()
                act.activation(work[:, 1, 128:128 + QR], latent[:, 0:QR], ACT.Square,
                               scale=QR ** -0.5, accum_out=ss_c[:, t, 0:1])
                act.activation(work[:, 1, 384:384 + KVR], latent[:, QR:], ACT.Square,
                               scale=KVR ** -0.5, accum_out=ss_c[:, t, 1:2]).then_inc(latent_ss, 1)
                act.activation(work[:, 3, 384:448], kpe[:, t, :], ACT.Square, scale=MLA_QK ** -0.5,
                               accum_out=ss_pe[:, t, :])
                act.activation(work[:].rearrange("p a b -> p (a b)")[:, 0:640], swa_raw[:], ACT.Square,
                               scale=SD ** -0.5).then_inc(swa_copied, 1)
                act.wait_ge(latent_psum, l * TB + (t + 1))
                act.activation(act_hi[:, t, 0:3, :], UV[t][:, 1, 0:384], ACT.Copy).then_inc(latent_hi_done, 1)

            def mla_parts(l, t):
                act.wait_ge(mla_done, l * TB + (t + 1))
                if t == 1:
                    act.wait_ge(mla_ss, l * TB + t)
                flat = work[:].rearrange("p a b -> p (a b)")
                act.activation(flat[:, 640:1152], UV[t][:, 0, :], ACT.Square, scale=MLA_QK ** -0.5)
                act.activation(flat[:, 1152:1664], A[t][:, 0, :], ACT.Square, scale=MLA_QK ** -0.5)
                act.activation(flat[:, 1664:1920], UV[t][:, 1, 0:256], ACT.Square, scale=MLA_QK ** -0.5)
                act.activation(v_mla[:, t, :], A[t][:, 1, :], ACT.Copy).then_inc(mla_squares, 1)

            def qk_copies(l, t):
                n = l * (5 * TB) + 5 * t
                act.wait_ge(qk_psum, n + 1)
                act.activation(qt[:, t, 0:4, :], A[t][:, 0, :], ACT.Copy, scale=cgain[:, 0:1]).then_inc(qk_act, 1)
                act.wait_ge(qk_psum, n + 3)
                act.activation(kt[:, 2:6, t, :], heads(UV[t][:, 0, :], 4), ACT.Copy, scale=cgain[:, 1:2]
                               ).then_inc(qk_act, 1)
                act.wait_ge(qk_psum, n + 5)
                act.activation(kt[:, 6, t, :], A[t][:, 0, 0:P], ACT.Copy).then_inc(qk_act, 1)

            def softmax(l, t):
                for b, (latent_heads, hs) in enumerate(BANKS[t]):
                    n = bank_no(l, t, b)
                    wide = (t + 1) * P
                    act.wait_ge(shift_ready, n + 1)
                    for j, hd in enumerate(hs):
                        col = hd if latent_heads else MH + hd
                        last = act.activation(probs[:, b % 2, j * wide:(j + 1) * wide],
                                              A[t][:, b % 2, j * wide:(j + 1) * wide], ACT.Exp,
                                              bias=shift[:, b % 2, j:j + 1],
                                              scale=MLA_SCALE if latent_heads else SWA_SCALE,
                                              accum_out=den[:, t, col:col + 1])
                    if not latent_heads:
                        last = act.activation(sink_e[:, t, hs[0]:hs[-1] + 1], sink_gap[:, t, hs[0]:hs[-1] + 1],
                                              ACT.Exp)
                    last.then_inc(probs_ready, 1)

            with act.Fori(0, DEPTH) as l:
                split(l, 0)
                split(l, 1)
                ffn(l, 0)
                split(l, MIX_AT + 2)
                for t in range(TB):
                    norm_squares(l, 1, t)
                    norm_hi(l, 1, t)
                    split(l, MIX_AT + 3 + t)
                split(l, MIX_AT + 5)
                act.wait_ge(small_loaded, l * 32 + 32)
                latent_and_window(l, 0)
                latent_and_window(l, 1)
                mla_parts(l, 0)
                split(l, MIX_AT + 6)
                split(l, MIX_AT + 7)
                qk_copies(l, 0)
                mla_parts(l, 1)
                split(l, MIX_AT + 8)
                split(l, MIX_AT + 9)
                qk_copies(l, 1)
                softmax(l, 0)
                norm_squares(l, 2, 0)
                norm_hi(l, 2, 0)
                split(l, FFN_AT[1])
                split(l, FFN_AT[1] + 1)
                softmax(l, 1)
                norm_squares(l, 2, 1)
                norm_hi(l, 2, 1)
                ffn(l, 1)

        @block.vector
        def _(dve):
            def split(l, unit, i=0, di=0):
                for half in range(2):
                    n = 2 * unit + half
                    dve.wait_ge(hi_done, l * (2 * LU) + i * (2 * di) + (n + 1))
                    dve.tensor_tensor(wlo_half(unit, half), raw[:, n % RAW, :],
                                      whi_half(unit, half).bitcast(F32), ALU.subtract).then_inc(split_done, 1)

            def add_to_x(l, s, t):
                dve.wait_ge(sum_ready, l * 6 + (2 * s + t + 1))
                dve.scalar_tensor_tensor(x[:, t, :], A[t][:].rearrange("p a b -> p (a b)"),
                                         1.0 if s == 1 else 0.5, x[:, t, :], ALU.mult, ALU.add
                                         ).then_inc(x_ready, 1)

            def norm_apply(l, k, t):
                n = 2 * k + t
                if t == 0:
                    dve.wait_ge(gain_loaded[k % 2], l * 32 + 16 * (k // 2 + 1))
                dve.wait_ge(rstd_ready, l * 8 + (n + 1))
                if n:
                    dve.wait_ge(xt_ready, l * 16 + 2 * n)
                if k == 2:
                    for seg in range(2):
                        w = slice(seg * 512, (seg + 1) * 512)
                        last = dve.scalar_tensor_tensor(xn[:, w], attn[:, w], rs_x[:, t, seg:seg + 1],
                                                        gain[:, 0, w], ALU.mult, ALU.mult)
                else:
                    last = dve.scalar_tensor_tensor(xn[:], x[:, t, :], rs_x[:, t, 0:1], gain[:, k % 2, :],
                                                    ALU.mult, ALU.mult)
                last.then_inc(xn_ready, 1)

            def norm_lo(l, k, t):
                for b in range(2):
                    dve.wait_ge(act_hi_done, l * 16 + (4 * k + 2 * t + b + 1))
                    last = dve.tensor_tensor(act_lo[:, t, 4 * b:4 * b + 4, :], heads(UV[t][:, b, :], 4),
                                             act_hi[:, t, 4 * b:4 * b + 4, :].bitcast(F32), ALU.subtract)
                last.then_inc(act_ready, 1)

            def ffn_group(l, f, g, i=0):
                n = l * (4 * NG) + i * 2 + (2 * (NG * f + g) + 1)

                def gate_times_up(t):
                    dve.wait_ge(silu_done, n + t)
                    dve.tensor_tensor(h[:, t, :], silu[:, t, :], UV[t][:, 0, GC:2 * GC], ALU.mult
                                      ).then_inc(h_ready, 1)

                def ht_low(t):
                    dve.wait_ge(ht_hi_done, n + t)
                    dve.tensor_tensor(ht_lo[:, t], heads(UV[t][:, 1, 0:GC], 2), ht_hi[:, t].bitcast(F32),
                                      ALU.subtract).then_inc(ht_ready, 1)

                gate_times_up(0)
                split(l, FFN_AT[f] + down_unit(g), i, 3)
                if g == NG - 1 and f == 0:
                    split(l, MIX_AT + 0)
                    split(l, MIX_AT + 1)
                gate_times_up(1)
                ht_low(0)
                if g + 2 < NG:
                    split(l, FFN_AT[f] + up_unit(g + 2), i, 3)
                    split(l, FFN_AT[f] + up_unit(g + 2) + 1, i, 3)
                ht_low(1)

            def ffn(l, f):
                k = 3 * f
                for t in range(TB):
                    if f == 1:
                        add_to_x(l, 1, t)
                    norm_apply(l, k, t)
                    norm_lo(l, k, t)
                split(l, FFN_AT[f] + 2)
                split(l, FFN_AT[f] + 3)
                ffn_group(l, f, 0)
                with dve.Fori(0, NG - 3, 2) as i:
                    ffn_group(l, f, 1, i)
                    ffn_group(l, f, 2, i)
                ffn_group(l, f, NG - 2)
                ffn_group(l, f, NG - 1)

            def rotate(src, first, n, t, ready):
                dst = heads(qkn[:, first:first + n // 2, :].rearrange("p a b -> p (a b)"), n)
                src, tmp = heads(src, n), heads(rot_tmp[:, 0:n * ROPE], n)
                hf = ROPE // 2
                dve.tensor_tensor(dst, src, over_heads(cs[:, t, 0, :], n), ALU.mult)
                dve.tensor_tensor(tmp[:, :, 0:hf], src[:, :, hf:ROPE], over_heads(cs[:, t, 1, 0:hf], n), ALU.mult)
                dve.tensor_tensor(tmp[:, :, hf:ROPE], src[:, :, 0:hf], over_heads(cs[:, t, 1, hf:ROPE], n),
                                  ALU.mult)
                dve.drain()
                last = dve.tensor_tensor(dst, dst, tmp, ALU.add)
                if ready:
                    last.then_inc(qkn_ready, 1)

            def latent_norm(l, t):
                dve.wait_ge(latent_rstd, l * TB + (t + 1))
                dve.wait_ge(xt_ready, l * 16 + 8)
                dve.scalar_tensor_tensor(xn[:, 0:QR], latent[:, 0:QR], rs_c[:, t, 0:1],
                                         sgain[:, SG_QA:SG_QA + QR], ALU.mult, ALU.mult)
                dve.scalar_tensor_tensor(xn[:, QR:QR + KVR], latent[:, QR:], rs_c[:, t, 1:2],
                                         sgain[:, SG_KVA:SG_KVA + KVR], ALU.mult, ALU.mult
                                         ).then_inc(latent_ready, 1)

            def window_norm(l, t):
                dve.wait_ge(swa_copied, l * TB + (t + 1))
                flat = work[:].rearrange("p a b -> p (a b)")
                dve.reduce_sum(ss_s[:, t, :], heads(flat[:, 0:640], 10), axis=AX_X).then_inc(swa_ss, 1)
                dve.wait_ge(swa_rstd, l * TB + (t + 1))
                dve.tensor_tensor(heads(rot_in, 10), heads(swa_raw[:], 10), spread(rs_s[:, t, :], SD), ALU.mult
                                  ).then_inc(swa_used, 1)
                dve.drain()
                q, k = heads(rot_in[:, 0:512], SH), heads(rot_in[:, 512:640], SKV)
                dve.tensor_tensor(q, q, over_heads(sgain[:, SG_SQ:SG_SQ + SD], SH), ALU.mult)
                dve.tensor_tensor(k, k, over_heads(sgain[:, SG_SK:SG_SK + SD], SKV), ALU.mult)
                dve.drain()
                if t == 1:
                    dve.wait_ge(qk_psum, l * (5 * TB) + 5)
                rotate(rot_in, CSQ, 10, t, False)

            def latent_lo(l, t):
                dve.wait_ge(latent_hi_done, l * TB + (t + 1))
                dve.tensor_tensor(act_lo[:, t, 0:3, :], heads(UV[t][:, 1, 0:384], 3),
                                  act_hi[:, t, 0:3, :].bitcast(F32), ALU.subtract).then_inc(latent_act, 1)

            def mla_norm(l, t):
                flat = work[:].rearrange("p a b -> p (a b)")
                dve.wait_ge(mla_squares, l * TB + (t + 1))
                dve.reduce_sum(ss_part[:, t, 0:8], heads(flat[:, 640:1664], 8), axis=AX_X)
                dve.reduce_sum(ss_part[:, t, 8:12], heads(flat[:, 1664:1920], 4), axis=AX_X)
                dve.drain()
                dve.tensor_tensor(ss_m[:, t, 0:4], ss_part[:, t, 0:4], ss_part[:, t, 8:12], ALU.add)
                dve.tensor_scalar(ss_m[:, t, 4:8], ss_part[:, t, 4:8], ss_pe[:, t, :], None, ALU.add
                                  ).then_inc(mla_ss, 1)
                dve.tensor_tensor(kpe_g[:], kpe[:, t, :], sgain[:, SG_MK:SG_MK + ROPE], ALU.mult)
                dve.drain()
                dve.wait_ge(mla_rstd, l * TB + (t + 1))
                q, k = heads(rot_in[:, 0:256], MH), heads(rot_in[:, 256:512], MH)
                dve.tensor_tensor(q, heads(UV[t][:, 1, 0:256], MH), spread(rs_m[:, t, 0:4], ROPE), ALU.mult)
                dve.tensor_tensor(k, over_heads(kpe_g[:], MH), spread(rs_m[:, t, 4:8], ROPE), ALU.mult)
                dve.drain()
                dve.tensor_tensor(q, q, over_heads(sgain[:, SG_MQ:SG_MQ + ROPE], MH), ALU.mult)
                dve.tensor_tensor(qkn[:, CQN:CQN + 4, :], heads(UV[t][:, 0, :], MH), spread(rs_m[:, t, 0:4], NOPE),
                                  ALU.mult)
                dve.tensor_tensor(qkn[:, CKN:CKN + 4, :], heads(A[t][:, 0, :], MH), spread(rs_m[:, t, 4:8], NOPE),
                                  ALU.mult)
                dve.drain()
                rotate(rot_in[:, 0:512], CQR, 8, t, True)

            def qk_copies(l, t):
                n = l * (5 * TB) + 5 * t
                dve.wait_ge(qk_psum, n + 2)
                dve.tensor_copy(qt[:, t, 4:6, :], heads(A[t][:, 1, 0:256], 2))
                dve.tensor_copy(kt[:, 0:2, t, :], heads(A[t][:, 1, 256:512], 2)).then_inc(qk_dve, 1)
                dve.wait_ge(qk_psum, n + 4)
                dve.tensor_copy(qt[:, t, 6:10, :], heads(UV[t][:, 1, :], 4)).then_inc(qk_dve, 1)

            def maxima(l, t, b):
                latent_heads, hs = BANKS[t][b]
                n, c = bank_no(l, t, b), len(hs)
                dve.wait_ge(scores_done, n + 1)
                dve.reduce_max(maxi[:, b % 2, 0:c], heads(A[t][:, b % 2, 0:c * (t + 1) * P], c), axis=AX_X)
                dve.drain()
                if latent_heads:
                    dve.tensor_scalar(shift[:, b % 2, 0:c], maxi[:, b % 2, 0:c], -MLA_SCALE, None, ALU.mult
                                      ).then_inc(shift_ready, 1)
                    return
                sink = sgain[:, SG_SINK + hs[0]:SG_SINK + hs[0] + c]
                dve.scalar_tensor_tensor(top[:, b % 2, 0:c], maxi[:, b % 2, 0:c], SWA_SCALE, sink, ALU.mult,
                                         ALU.max)
                dve.drain()
                dve.tensor_tensor(sink_gap[:, t, hs[0]:hs[0] + c], sink, top[:, b % 2, 0:c], ALU.subtract)
                dve.tensor_scalar(shift[:, b % 2, 0:c], top[:, b % 2, 0:c], -1.0, None, ALU.mult
                                  ).then_inc(shift_ready, 1)

            def probs_copy(l, t, b):
                dve.wait_ge(pt_psum, bank_no(l, t, b) + 1)
                w = len(BANKS[t][b][1]) * (t + 1) * P
                dve.tensor_copy(probs_t[:, b % 2, 0:w], UV[t][:, 0, 0:w]).then_inc(pt_ready, 1)

            def attention(l, t):
                last_latent = 1
                last = len(BANKS[t]) - 1
                for b in range(last + 2):
                    if b <= last:
                        maxima(l, t, b)
                    if b:
                        probs_copy(l, t, b - 1)
                    if b - 1 == last_latent:
                        dve.reciprocal(rden[:, t, 0:MH], den[:, t, 0:MH])
                        dve.drain()
                        dve.wait_ge(pv_done, bank_no(l, t, last_latent) + 1)
                        dve.tensor_tensor(heads(attn[:, 0:512], MH), heads(UV[t][:, 1, :], MH),
                                          spread(rden[:, t, 0:MH], MV), ALU.mult).then_inc(attn_ready, 1)
                dve.tensor_tensor(rden[:, t, MH:], den[:, t, MH:], sink_e[:, t, :], ALU.add)
                dve.drain()
                dve.reciprocal(rden[:, t, MH:], rden[:, t, MH:])
                dve.drain()
                dve.wait_ge(pv_done, bank_no(l, t, last) + 1)
                dve.tensor_tensor(heads(attn[:, 512:], SH), heads(UV[t][:, 1, :], SH),
                                  spread(rden[:, t, MH:], SD), ALU.mult).then_inc(attn_ready, 1)

            dve.memset(top[:], 0.0).then_inc(split_done, RAW)
            dve.wait_ge(x_loaded, 16 * TB)
            dve.memset(maxi[:], 0.0).then_inc(x_ready, TB)
            dve.wait_ge(rope_loaded, 16)
            with dve.Fori(0, DEPTH) as l:
                split(l, 0)
                split(l, 1)
                ffn(l, 0)
                split(l, MIX_AT + 2)
                for t in range(TB):
                    add_to_x(l, 0, t)
                    norm_apply(l, 1, t)
                    norm_lo(l, 1, t)
                    split(l, MIX_AT + 3 + t)
                split(l, MIX_AT + 5)
                dve.wait_ge(small_loaded, l * 32 + 32)
                latent_norm(l, 0)
                latent_lo(l, 0)
                window_norm(l, 0)
                latent_norm(l, 1)
                latent_lo(l, 1)
                mla_norm(l, 0)
                split(l, MIX_AT + 6)
                split(l, MIX_AT + 7)
                qk_copies(l, 0)
                window_norm(l, 1)
                mla_norm(l, 1)
                split(l, MIX_AT + 8)
                split(l, MIX_AT + 9)
                qk_copies(l, 1)
                attention(l, 0)
                norm_apply(l, 2, 0)
                norm_lo(l, 2, 0)
                split(l, FFN_AT[1])
                split(l, FFN_AT[1] + 1)
                attention(l, 1)
                norm_apply(l, 2, 1)
                norm_lo(l, 2, 1)
                ffn(l, 1)
                for t in range(TB):
                    add_to_x(l, 2, t)

        @block.tensor
        def _(pe):
            def halves_split(l, n, i=0):
                pe.wait_ge(split_done, l * (2 * LU) + i * 6 + (RAW + n + 1))

            def product(dst, hi, lo, w_hi, w_lo, start, stop):
                pe.matmul(dst, hi, w_hi, start=start, stop=False, skip_group_check=True)
                pe.matmul(dst, hi, w_lo, start=False, stop=False, skip_group_check=True)
                return pe.matmul(dst, lo, w_hi, start=False, stop=stop, skip_group_check=True)

            def transpose_norm(l, k, t, frees=False):
                pe.wait_ge(xn_ready, l * 8 + (2 * k + t + 1))
                for c in range(KD):
                    if c == 1 and frees:
                        last.then_inc(unit_freed, 1)
                    last = pe.transpose(UV[t][:, c // 4, (c % 4) * P:(c % 4 + 1) * P], xn[:, c * P:(c + 1) * P],
                                        ident[:])
                    if c % 4 == 3:
                        last.then_inc(xt_ready, 1)

            def up(l, f, g, t, part, i=0):
                if g and not part:
                    pe.wait_ge(h_ready, l * (4 * NG) + i * 2 + (2 * (NG * f + g - 1) + t + 1))
                unit = FFN_AT[f] + up_unit(g)
                for k in range(4 * part, 4 * part + 4):
                    if t == 0 and k % 2 == 0:
                        halves_split(l, 2 * unit + k // 2, i)
                    w = slice((k % 2) * 512, (k % 2 + 1) * 512)
                    u, hf = unit + k // 4, k // 2 % 2
                    last = product(UV[t][:, 0, :], act_hi[:, t, k, :], act_lo[:, t, k, :],
                                   whi_half(u, hf)[:, w], wlo_half(u, hf)[:, w], k == 0, k == KD - 1)
                if part:
                    last.then_inc(up_done, 1)
                return last

            def transpose_h(l, f, g, t, i=0):
                n = l * (4 * NG) + i * 2 + (2 * (NG * f + g) + t + 1)
                pe.wait_ge(h_ready, n)
                for c in range(2):
                    last = pe.transpose(UV[t][:, 1, c * P:(c + 1) * P], h[:, t, c * P:(c + 1) * P], ident[:])
                last.then_inc(ht_psum, 1)

            def down(l, f, g, t, i=0):
                unit = FFN_AT[f] + down_unit(g)
                pe.wait_ge(ht_ready, l * (4 * NG) + i * 2 + (2 * (NG * f + g) + t + 1))
                for c in range(2):
                    if t == 0:
                        halves_split(l, 2 * unit + c, i)
                    for n in range(2):
                        w = slice(n * 512, (n + 1) * 512)
                        last = product(A[t][:, n, :], ht_hi[:, t, c, :], ht_lo[:, t, c, :],
                                       whi_half(unit, c)[:, w], wlo_half(unit, c)[:, w],
                                       g == 0 and c == 0, g == NG - 1 and c == 1)
                return last

            def ffn_step(l, f, g, i=0):
                for t in range(TB):
                    last = up(l, f, g, t, 0, i)
                    if g == 1 and t == 0:
                        last.then_inc(unit_freed, 2)
                    transpose_h(l, f, g - 1, t, i)
                    up(l, f, g, t, 1, i)
                    last = down(l, f, g - 1, t, i)
                last.then_inc(unit_freed, 3)

            def ffn(l, f):
                for t in range(TB):
                    transpose_norm(l, 3 * f, t, t == 0)
                    pe.wait_ge(act_ready, l * 8 + (6 * f + t + 1))
                    up(l, f, 0, t, 0)
                    up(l, f, 0, t, 1)
                ffn_step(l, f, 1)
                with pe.Fori(0, NG - 3, 2) as i:
                    ffn_step(l, f, 2, i)
                    ffn_step(l, f, 3, i)
                ffn_step(l, f, NG - 1)
                for t in range(TB):
                    transpose_h(l, f, NG - 1, t)
                for t in range(TB):
                    down(l, f, NG - 1, t).then_inc(sum_ready, 1)

            def input_main(l, t, chunks):
                for k in chunks:
                    u, hf = MIX_AT + k // 2, k % 2
                    if t == 0:
                        halves_split(l, 2 * u + hf)
                    for n in range(2):
                        w = slice(n * 512, (n + 1) * 512)
                        last = product(A[t][:, n, :], act_hi[:, t, k, :], act_lo[:, t, k, :],
                                       whi_half(u, hf)[:, w], wlo_half(u, hf)[:, w], k == 0, k == KD - 1)
                return last

            def input_tail(l, t):
                for k in range(KD):
                    u, hf = MIX_AT + 4, k // 4
                    if t == 0 and k % 4 == 0:
                        halves_split(l, 2 * u + hf)
                    w = slice((k % 4) * 192, (k % 4 + 1) * 192)
                    last = product(UV[t][:, 0, 0:192], act_hi[:, t, k, :], act_lo[:, t, k, :],
                                   whi_half(u, hf)[:, w], wlo_half(u, hf)[:, w], k == 0, k == KD - 1)
                return last.then_inc(proj_done, 1)

            def transpose_latent(l, t):
                pe.wait_ge(latent_ready, l * TB + (t + 1))
                for c in range(3):
                    last = pe.transpose(UV[t][:, 1, c * P:(c + 1) * P], xn[:, c * P:(c + 1) * P], ident[:])
                last.then_inc(latent_psum, 1)

            def latent_products(l, t):
                pe.wait_ge(latent_act, l * TB + (t + 1))
                u = MIX_AT + 5
                if t == 0:
                    halves_split(l, 2 * u + 1)
                for n in range(2):
                    w = slice(n * 512, (n + 1) * 512)
                    product(A[t][:, n, :], act_hi[:, t, 2, :], act_lo[:, t, 2, :],
                            whi_half(u, 1)[:, w], wlo_half(u, 1)[:, w], True, True)
                for k in range(2):
                    w = slice(k * 512, (k + 1) * 512)
                    product(UV[t][:, 0, :], act_hi[:, t, k, :], act_lo[:, t, k, :],
                            whi_half(u, 0)[:, w], wlo_half(u, 0)[:, w], k == 0, k == 1)
                for k in range(2):
                    w = slice(768, 1024)
                    last = product(UV[t][:, 1, 0:256], act_hi[:, t, k, :], act_lo[:, t, k, :],
                                   whi_half(u - 1, k)[:, w], wlo_half(u - 1, k)[:, w], k == 0, k == 1)
                return last.then_inc(mla_done, 1)

            def transpose_qk(l, t):
                n = l * (5 * TB) + 5 * t
                pe.wait_ge(qkn_ready, l * TB + (t + 1))
                banks = [A[t][:, 0, :], A[t][:, 1, :], UV[t][:, 0, :], UV[t][:, 1, :], A[t][:, 0, :]]
                for b, bank in enumerate(banks):
                    if b == 4:
                        pe.wait_ge(qk_act, l * (3 * TB) + (3 * t + 1))
                    for c in range(4 * b, min(4 * b + 4, CHUNKS)):
                        last = pe.transpose(bank[:, (c % 4) * P:(c % 4 + 1) * P], qkn[:, c, :], ident[:])
                        if t == 0 and c == 0:
                            last.then_inc(unit_freed, 2)
                    last.then_inc(qk_psum, 1)

            def scores(l, t, b):
                latent_heads, hs = BANKS[t][b]
                n, wide = bank_no(l, t, b), (t + 1) * P
                if b >= 2:
                    pe.wait_ge(probs_ready, n - 1)
                for j, hd in enumerate(hs):
                    dst = A[t][:, b % 2, j * wide:(j + 1) * wide]
                    if latent_heads:
                        r = ROPE * (hd % 2)
                        pe.matmul(dst, qt[:, t, hd, :], kt[:, 2 + hd, 0:t + 1, :], start=True, stop=False,
                                  skip_group_check=True)
                        pe.matmul(dst, qt[r:r + ROPE, t, 4 + hd // 2, :], kt[r:r + ROPE, hd // 2, 0:t + 1, :],
                                  start=False, stop=False, skip_group_check=True)
                        last = pe.matmul(dst[:, t * P:wide], ident_b[:], masks[:, 1, :], start=False, stop=True,
                                         skip_group_check=True)
                    else:
                        r = SD * (hd // 4)
                        pe.matmul(dst, qt[r:r + SD, t, 6 + hd % 4, :], kt[r:r + SD, 6, 0:t + 1, :], start=True,
                                  stop=False, skip_group_check=True)
                        last = pe.matmul(dst, ident_b[:], masks[:, 1 - t:2, :], start=False, stop=True,
                                         skip_group_check=True)
                last.then_inc(scores_done, 1)

            def values(l, t, b):
                latent_heads, hs = BANKS[t][b]
                n = bank_no(l, t, b)
                pe.wait_ge(probs_ready, n + 1)
                for c in range(len(hs) * (t + 1)):
                    last = pe.transpose(UV[t][:, 0, c * P:(c + 1) * P], probs[:, b % 2, c * P:(c + 1) * P], ident[:])
                last.then_inc(pt_psum, 1)
                pe.wait_ge(pt_ready, n + 1)
                if not latent_heads and hs[0] == 0:
                    pe.wait_ge(attn_ready, l * 4 + (2 * t + 1))
                for j, hd in enumerate(hs):
                    for c in range(t + 1):
                        if latent_heads:
                            dst, v = UV[t][:, 1, hd * MV:(hd + 1) * MV], v_mla[:, c, hd * MV:(hd + 1) * MV]
                        else:
                            kv = hd // (SH // SKV)
                            dst, v = UV[t][:, 1, hd * SD:(hd + 1) * SD], v_swa[:, c, kv * SD:(kv + 1) * SD]
                        last = pe.matmul(dst, probs_t[:, b % 2, (j * (t + 1) + c) * P:(j * (t + 1) + c + 1) * P], v,
                                         start=c == 0, stop=c == t, skip_group_check=True)
                last.then_inc(pv_done, 1)

            def output_chunk(l, t, k):
                u, hf = MIX_AT + 6 + k // 2, k % 2
                if t == 0:
                    halves_split(l, 2 * u + hf)
                for n in range(2):
                    w = slice(n * 512, (n + 1) * 512)
                    last = product(A[t][:, n, :], act_hi[:, t, k, :], act_lo[:, t, k, :],
                                   whi_half(u, hf)[:, w], wlo_half(u, hf)[:, w], k == 0, k == KD - 1)
                if k == KD - 1:
                    last.then_inc(sum_ready, 1)
                elif k % 2 and t == 1:
                    last.then_inc(unit_freed, 1)

            pe.wait_ge(const_ready, 1)
            with pe.Fori(0, DEPTH) as l:
                ffn(l, 0)
                transpose_norm(l, 1, 0, True)
                pe.wait_ge(act_ready, l * 8 + 3)
                input_main(l, 0, range(0, 5))
                transpose_norm(l, 1, 1)
                input_main(l, 0, range(5, KD))
                input_tail(l, 0)
                pe.wait_ge(act_ready, l * 8 + 4)
                input_main(l, 1, range(0, 4))
                transpose_latent(l, 0)
                input_main(l, 1, range(4, KD)).then_inc(unit_freed, 4)
                input_tail(l, 1)
                latent_products(l, 0)
                transpose_latent(l, 1)
                latent_products(l, 1)
                transpose_qk(l, 0)
                transpose_qk(l, 1)
                pe.wait_ge(qk_act, l * (3 * TB) + 3)
                pe.wait_ge(qk_dve, l * (2 * TB) + 2)
                for b in range(len(BANKS[0]) + 1):
                    if b < len(BANKS[0]):
                        scores(l, 0, b)
                    if b:
                        values(l, 0, b - 1)
                transpose_norm(l, 2, 0)
                pe.wait_ge(act_ready, l * 8 + 5)
                pe.wait_ge(qk_act, l * (3 * TB) + 6)
                pe.wait_ge(qk_dve, l * (2 * TB) + 4)
                for b in range(KD):
                    if b < len(BANKS[1]):
                        scores(l, 1, b)
                    output_chunk(l, 0, b)
                    if 1 <= b <= len(BANKS[1]):
                        values(l, 1, b - 1)
                transpose_norm(l, 2, 1)
                pe.wait_ge(act_ready, l * 8 + 6)
                for b in range(KD):
                    output_chunk(l, 1, b)
                ffn(l, 1)


def kernel(**inputs):
    import numpy as np
    import concourse.bacc as bacc
    from concourse.bass_utils import run_bass_kernel_spmd as run

    a = {n: np.ascontiguousarray(v) for n, v in inputs.items()}

    def halves(l):
        out = []

        def up(f, g):
            w = [a[f"ffn{f + 1}_w_{n}"][l][:, g * GC:(g + 1) * GC].reshape(KD // 2, 2, P, GC)
                 for n in ("gate", "up")]
            out.extend(np.stack(w, 3).transpose(0, 2, 1, 3, 4).reshape(KD // 2, P, HC))

        def down(f, g):
            out.extend(a[f"ffn{f + 1}_w_down"][l][g * GC:(g + 1) * GC].reshape(2, P, HC))

        def ffn(f):
            up(f, 0)
            up(f, 1)
            for g in range(NG):
                down(f, g)
                if g + 2 < NG:
                    up(f, g + 2)

        ffn(0)
        w = a["w_in"][l]
        at = np.cumsum([0, QR, KVR, ROPE, SH * SD, SKV * SD, SKV * SD])
        cq, ckv, kpe, qs, ks, vs = (w[:, at[j]:at[j + 1]] for j in range(6))
        qs = qs.reshape(D, SKV, SH // SKV, SD).transpose(0, 2, 1, 3).reshape(D, SH * SD)
        out.extend(np.concatenate([cq, ckv, ks, qs], 1).reshape(KD, P, HC))
        tail = np.concatenate([vs, kpe], 1).reshape(2, 4, P, 192).transpose(0, 2, 1, 3).reshape(2, P, 768)
        qb = a["mla_w_q_b"][l].reshape(2, P, MH, MLA_QK)
        q_nope, q_rope = qb[..., :NOPE].reshape(2, P, 512), qb[..., NOPE:].reshape(2, P, 256)
        out.extend(np.concatenate([tail, q_rope], 2))
        out.append(q_nope.transpose(1, 0, 2).reshape(P, HC))
        out.append(a["mla_w_kv_b"][l].reshape(P, MH, 2, P).transpose(0, 2, 1, 3).reshape(P, HC))
        out.extend(a["w_o"][l].reshape(KD, P, HC))
        ffn(1)
        return out

    f32 = np.float32
    stream = np.stack([t for l in range(DEPTH) for t in halves(l)])
    norm_gains = np.stack([g for l in range(DEPTH) for g in (
        a["ffn1_norm"][l], a["mix_norm"][l], np.concatenate([a["mla_out_norm"][l], a["swa_out_norm"][l]]),
        a["ffn2_norm"][l])])
    small = np.concatenate([a["mla_q_a_norm"], a["mla_kv_a_norm"], a["swa_q_norm"], a["swa_k_norm"],
                            a["mla_q_norm"][:, NOPE:], a["mla_k_norm"][:, NOPE:], a["swa_sinks"]], 1)
    cols = np.ascontiguousarray(np.stack([a["mla_q_norm"][:, :NOPE], a["mla_k_norm"][:, :NOPE]], 2))
    inv = 1.0 / (f32(10000.0) ** (np.arange(0, ROPE, 2, dtype=f32) / f32(ROPE)))
    angle = np.arange(SEQ, dtype=f32)[:, None] * inv[None, :].astype(f32)
    c, s = np.cos(angle).astype(f32), np.sin(angle).astype(f32)
    rope = np.stack([np.concatenate([c, c], 1), np.concatenate([-s, s], 1)], 1).reshape(TB, P, 2, ROPE)

    arrays = {"x_in": a["x"].reshape(SEQ, D), "stream": stream, "norm_gains": norm_gains, "small_gains": small,
              "col_gains": cols, "rope": np.ascontiguousarray(rope)}
    nc = bacc.Bacc("TRN2", target_bir_lowering=False, num_devices=1)
    args = [nc.dram_tensor(n, v.shape, F32, kind="ExternalInput").ap() for n, v in arrays.items()]
    result = nc.dram_tensor("out", (SEQ, D), F32, kind="ExternalOutput").ap()
    hybrid_trunk(nc, *args, result)
    r = run(nc, [arrays], core_ids=[0])
    return r.results[0]["out"].reshape(1, SEQ, D)
```

```python
from contextlib import ExitStack

import concourse.bass as bass
from concourse import mybir

ALU = mybir.AluOpType
ACT = mybir.ActivationFunctionType
AX_X = mybir.AxisListType.X
F32 = mybir.dt.float32
F32R = mybir.dt.float32r
BF16 = mybir.dt.bfloat16

P = 128
D = 1024
SEQ = 256
DEPTH = 2
TB = SEQ // P
KD = D // P
EPS = 1e-6
FF = 2816
GC = 256
NG = FF // GC
QR, KVR = 256, 128
MH, NOPE, ROPE, MV = 4, 128, 64, 128
SH, SKV, SD = 8, 2, 64
MLA_QK = NOPE + ROPE
MLA_SCALE = MLA_QK ** -0.5
SWA_SCALE = SD ** -0.5
MASKED = -1e30

RAW = 4
UNITS = 6
HC = 1024
FFN_UNITS = 3 * NG
MIX_UNITS = 10
LU = 2 * FFN_UNITS + MIX_UNITS
FFN_AT = (-1, FFN_UNITS - 1 + MIX_UNITS)
MIX_AT = FFN_UNITS - 1
NEXT_UNIT = LU - 1
NORMS = 4

SG_QA, SG_KVA = 0, QR
SG_SQ = QR + KVR
SG_SK, SG_MQ, SG_MK, SG_SINK = SG_SQ + 64, SG_SQ + 128, SG_SQ + 192, SG_SQ + 256
SG = SG_SINK + SH

CQN, CQR, CKR, CKN, CSQ, CSK, CHUNKS = 0, 4, 6, 8, 12, 16, 17


def half_no(unit, half):
    return 2 * (unit + 1) + half


def up_unit(g):
    return 2 * g if g < 2 else 3 * g - 1


def down_unit(g):
    return 4 + 3 * g if g < NG - 1 else FFN_UNITS - 1


def unit_slots():
    def ffn(first):
        slots = [None] * FFN_UNITS
        for g in range(NG):
            base = (first + 3 * g) % UNITS
            slots[up_unit(g)], slots[up_unit(g) + 1], slots[down_unit(g)] = base, base + 1, base + 2
        return slots

    slots = ffn(0) + [3, 4, 0, 1, 5, 2, 3, 4, 0, 1] + ffn(3)
    twice = slots + slots
    back = {}
    for u in range(LU, 2 * LU):
        last = max(v for v in range(u) if twice[v] == twice[u])
        back[u - LU - 1] = min(u - last, UNITS)
    slot = {u - 1: slots[u] for u in range(LU)}
    slot[NEXT_UNIT], back[NEXT_UNIT] = slot[-1], back[-1]
    return slot, back


SLOT, BACK = unit_slots()


def hybrid_trunk(nc, x_in, stream, norm_gains, small_gains, col_gains, rope, out):
    with ExitStack() as ctx:
        def sb(name, shape, dt=F32):
            return ctx.enter_context(nc.sbuf_tensor(name, shape, dt))

        def pb(name, shape):
            return ctx.enter_context(nc.psum_tensor(name, shape, F32))

        def sem(name):
            return ctx.enter_context(nc.semaphore(name))

        def heads(ap, n):
            return ap.rearrange("p (n d) -> p n d", n=n)

        raw = sb("raw", [P, RAW, HC])
        whi = sb("whi", [P, UNITS, 2 * HC], F32R)
        wlo = sb("wlo", [P, UNITS, 2 * HC], F32R)
        x = sb("x", [P, TB, D])
        act_hi = sb("act_hi", [P, TB, KD, P], F32R)
        act_lo = sb("act_lo", [P, TB, KD, P], F32R)
        gain = sb("gain", [P, 2, D])
        sgain = sb("sgain", [P, SG])
        cgain = sb("cgain", [P, 2])
        cs = sb("cs", [P, TB, 2, ROPE])
        xn = sb("xn", [P, D])
        rot = sb("rot", [P, 2 * 640])
        rot_in, rot_tmp = rot[:, 0:640], rot[:, 640:1280]
        attn = sb("attn", [P, D])
        latent, swa_raw = attn[:, 0:384], attn[:, 384:D]
        ht_hi = sb("ht_hi", [P, TB, 2, P], F32R)
        ht_lo = sb("ht_lo", [P, TB, 2, P], F32R)
        work = sb("work", [P, 4, 512])
        silu = heads(work[:, 0, :], TB)
        h = heads(work[:, 1, :], TB)
        probs = work[:, 0:2, :]
        probs_t = work[:, 2:4, :]
        kpe = sb("kpe", [P, TB, ROPE])
        kpe_g = sb("kpe_g", [P, ROPE])
        qkn = sb("qkn", [P, CHUNKS, P])
        squares = qkn[:].rearrange("p a b -> p (a b)")
        qt = sb("qt", [P, TB, 10, P])
        kt = sb("kt", [P, 7, TB, P])
        v_mla = sb("v_mla", [P, TB, MH * MV])
        v_swa = sb("v_swa", [P, TB, SKV * SD])
        ident = sb("ident", [P, P])
        ident_b = sb("ident_b", [P, P], BF16)
        masks = sb("masks", [P, 2, P], BF16)
        consts = sb("consts", [P, 2, 16])
        ss_x = sb("ss_x", [P, TB, 2])
        rs_x = sb("rs_x", [P, TB, 2])
        ss_c = sb("ss_c", [P, TB, 2])
        rs_c = sb("rs_c", [P, TB, 2])
        ss_s = sb("ss_s", [P, TB, 10])
        rs_s = sb("rs_s", [P, TB, 10])
        ss_part = sb("ss_part", [P, TB, 12])
        ss_pe = sb("ss_pe", [P, TB, 1])
        ss_m = sb("ss_m", [P, TB, 8])
        rs_m = sb("rs_m", [P, TB, 8])
        top = sb("top", [P, 2, 4])
        shift = sb("shift", [P, 2, 4])
        sink_gap = sb("sink_gap", [P, TB, SH])
        sink_e = sb("sink_e", [P, TB, SH])
        den = sb("den", [P, TB, MH + SH])
        rden = sb("rden", [P, TB, MH + SH])
        maxi = sb("maxi", [P, 2, 4])

        UV = [pb(f"UV{t}", [P, 2, 512]) for t in range(TB)]
        A = [pb(f"A{t}", [P, 2, 512]) for t in range(TB)]

        raw_landed = [sem(f"raw_landed{r}") for r in range(RAW)]
        hi_done = sem("hi_done")
        split_done = sem("split_done")
        unit_freed = sem("unit_freed")
        x_loaded = [sem("x_loaded0"), sem("x_loaded1")]
        rope_loaded = sem("rope_loaded")
        gain_loaded = [sem("gain_loaded0"), sem("gain_loaded1")]
        small_loaded = sem("small_loaded")
        const_ready = sem("const_ready")
        pool_step = sem("pool_step")
        x_ready = sem("x_ready")
        ss_ready = sem("ss_ready")
        rstd_ready = sem("rstd_ready")
        xn_ready = sem("xn_ready")
        xt_ready = sem("xt_ready")
        act_hi_done = sem("act_hi_done")
        act_ready = sem("act_ready")
        up_done = sem("up_done")
        silu_done = sem("silu_done")
        h_ready = sem("h_ready")
        ht_psum = sem("ht_psum")
        ht_hi_done = sem("ht_hi_done")
        ht_ready = sem("ht_ready")
        sum_ready = sem("sum_ready")
        proj_done = sem("proj_done")
        latent_ss = sem("latent_ss")
        latent_rstd = sem("latent_rstd")
        latent_ready = sem("latent_ready")
        latent_psum = sem("latent_psum")
        latent_hi_done = sem("latent_hi_done")
        latent_act = sem("latent_act")
        swa_copied = sem("swa_copied")
        swa_ss = sem("swa_ss")
        swa_rstd = sem("swa_rstd")
        swa_used = sem("swa_used")
        mla_done = sem("mla_done")
        mla_squares = sem("mla_squares")
        mla_ss = sem("mla_ss")
        mla_rstd = sem("mla_rstd")
        qkn_ready = sem("qkn_ready")
        qk_psum = sem("qk_psum")
        qk_act = sem("qk_act")
        qk_dve = sem("qk_dve")
        scores_done = sem("scores_done")
        shift_ready = sem("shift_ready")
        probs_ready = sem("probs_ready")
        pt_psum = sem("pt_psum")
        pt_ready = sem("pt_ready")
        pv_done = sem("pv_done")
        attn_ready = sem("attn_ready")
        stored = sem("stored")

        def whi_half(unit, half):
            return whi[:, SLOT[unit], half * HC:(half + 1) * HC]

        def wlo_half(unit, half):
            return wlo[:, SLOT[unit], half * HC:(half + 1) * HC]

        def spread(ap, n):
            return ap.unsqueeze(2).to_broadcast([P, ap.shape[1], n])

        def over_heads(ap, n):
            return ap.unsqueeze(1).to_broadcast([P, n, ap.shape[1]])

        def score_banks(t):
            per = 4 // (t + 1)
            return [(True, [0, 2]), (True, [1, 3])] + [(False, list(range(i, i + per))) for i in range(0, SH, per)]

        BANKS = [score_banks(t) for t in range(TB)]
        LB = len(BANKS[0]) + len(BANKS[1])

        def bank_no(l, t, b):
            return l * LB + (len(BANKS[0]) if t else 0) + b

        block = ctx.enter_context(nc.Block())

        @block.sync
        def _(sp):
            sp.dma_start(x[:, 0, :], x_in[0:P, :]).then_inc(x_loaded[0], 16)
            with sp.Fori(0, DEPTH * LU * 2 // RAW) as i:
                for r in range(RAW):
                    sp.wait_ge(split_done, i * RAW + (r + 1))
                    sp.dma_start(raw[:, r, :], stream[bass.ds(i * RAW + r, 1)].rearrange("a p n -> (a p) n")
                                 ).then_inc(raw_landed[r], 16)
            for r in range(2):
                sp.wait_ge(split_done, DEPTH * LU * 2 + r + 1)
                sp.dma_start(raw[:, r, :], stream[r]).then_inc(raw_landed[r], 16)
            for t in range(TB):
                sp.wait_ge(x_ready, DEPTH * 6 + t + 1)
                sp.dma_start(out[t * P:(t + 1) * P, :], x[:, t, :]).then_inc(stored, 16)
            sp.wait_ge(stored, 16 * TB)

        @block.gpsimd
        def _(pool):
            def load_gain(l, k):
                src = norm_gains[bass.ds(l * NORMS + k, 1), :].to_broadcast([P, D])
                pool.dma_start(gain[:, k % 2, :], src).then_inc(gain_loaded[k % 2], 16)

            load_gain(0, 0)
            pool.dma_start(x[:, 1, :], x_in[P:2 * P, :]).then_inc(x_loaded[1], 16)
            pool.memset(consts[:, 1, :], EPS)
            pool.memset(consts[:, 0, :], -0.5).then_inc(unit_freed, UNITS - 1)
            pool.memset(ident[:], 0.0)
            pool.memset(ident_b[:], 0.0)
            pool.memset(masks[:], 0.0).then_inc(pool_step, 1)
            pool.wait_ge(pool_step, 1)
            for m in (ident, ident_b):
                pool.affine_select(out=m[:], in_=m[:], compare_op=ALU.not_equal, fill=1.0, base=0,
                                   pattern=[[-1, P]], channel_multiplier=1)
            pool.affine_select(out=masks[:, 0, :], in_=masks[:, 0, :], compare_op=ALU.is_gt, fill=MASKED,
                               base=0, pattern=[[1, P]], channel_multiplier=-1)
            pool.affine_select(out=masks[:, 1, :], in_=masks[:, 1, :], compare_op=ALU.is_ge, fill=MASKED,
                               base=0, pattern=[[-1, P]], channel_multiplier=1).then_inc(const_ready, 1)

            def rstd(l, rs, ms, ready, n):
                pool.tensor_tensor(rs, ms, consts[:, 1, 0:ms.shape[1]], ALU.add).then_inc(pool_step, 1)
                pool.wait_ge(pool_step, l * 14 + (n + 2))
                pool.tensor_tensor(rs, rs, consts[:, 0, 0:ms.shape[1]], ALU.pow).then_inc(ready, 1)

            def norm_rstd(l, k, t):
                pool.wait_ge(ss_ready, l * 8 + (2 * k + t + 1))
                w = 2 if k == 2 else 1
                rstd(l, rs_x[:, t, 0:w], ss_x[:, t, 0:w], rstd_ready, 2 * k + t + (6 if k > 1 else 0))

            norm_rstd(0, 0, 0)
            pool.dma_start(cs[:], rope.rearrange("t p a d -> p t a d")).then_inc(rope_loaded, 16)
            with pool.Fori(0, DEPTH) as l:
                pool.dma_start(sgain[:], small_gains[bass.ds(l, 1), :].to_broadcast([P, SG])
                               ).then_inc(small_loaded, 16)
                pool.dma_start(cgain[:], col_gains[bass.ds(l, 1)].rearrange("a p c -> (a p) c")
                               ).then_inc(small_loaded, 16)
                load_gain(l, 1)
                norm_rstd(l, 0, 1)
                pool.wait_ge(xn_ready, l * 16 + 4)
                load_gain(l, 2)
                norm_rstd(l, 1, 0)
                norm_rstd(l, 1, 1)
                pool.wait_ge(xn_ready, l * 16 + 8)
                load_gain(l, 3)
                def latent(t):
                    pool.wait_ge(latent_ss, l * TB + (t + 1))
                    rstd(l, rs_c[:, t, :], ss_c[:, t, :], latent_rstd, 4 + 3 * t)

                def window(t):
                    pool.wait_ge(swa_ss, l * TB + (t + 1))
                    rstd(l, rs_s[:, t, :], ss_s[:, t, :], swa_rstd, 5 + 3 * t)

                def mla(t):
                    pool.wait_ge(mla_ss, l * TB + (t + 1))
                    rstd(l, rs_m[:, t, :], ss_m[:, t, :], mla_rstd, 6 + 3 * t)

                for t in range(TB):
                    latent(t)
                    window(t)
                    mla(t)
                for k in (2, 3):
                    for t in range(TB):
                        norm_rstd(l, k, t)
                    if k == 2:
                        pool.wait_ge(xn_ready, l * 16 + 12)
                        load_gain(l, 4)
                norm_rstd(l, 4, 0)

        @block.scalar
        def _(act):
            def split(l, unit, i=0, di=0):
                for half in range(2):
                    n = half_no(unit, half)
                    act.wait_ge(raw_landed[n % RAW], l * (16 * 2 * LU // RAW) + i * (16 * 2 * di // RAW)
                                + 16 * (n // RAW + 1))
                    if half == 0:
                        act.wait_ge(unit_freed, l * LU + i * di + (unit + 1 - BACK[unit] + 1 + UNITS))
                    act.activation(whi_half(unit, half), raw[:, n % RAW, :], ACT.Copy).then_inc(hi_done, 1)

            def norm_squares(l, k, t):
                if k == 2:
                    act.wait_ge(attn_ready, l * 4 + (2 * t + 2))
                    for seg in range(2):
                        sq = act.activation(UV[t][:, seg, :], attn[:, seg * 512:(seg + 1) * 512], ACT.Square,
                                            scale=(D // 2) ** -0.5, accum_out=ss_x[:, t, seg:seg + 1])
                else:
                    act.wait_ge(x_ready, l * 6 + (2 * {0: 0, 1: 1, 3: 2, 4: 3}[k] + t + 1))
                    sq = act.activation(UV[t][:].rearrange("p a b -> p (a b)"), x[:, t, :], ACT.Square,
                                        scale=D ** -0.5, accum_out=ss_x[:, t, 0:1])
                sq.then_inc(ss_ready, 1)

            def norm_hi(l, k, t):
                for b in range(2):
                    act.wait_ge(xt_ready, l * 16 + (4 * k + 2 * t + b + 1))
                    act.activation(act_hi[:, t, 4 * b:4 * b + 4, :], UV[t][:, b, :], ACT.Copy
                                   ).then_inc(act_hi_done, 1)

            def ffn_group(l, f, g, i=0):
                n = l * (4 * NG) + i * 2 + (2 * (NG * f + g) + 1)

                def silu_block(t):
                    act.wait_ge(up_done, n + t)
                    act.activation(silu[:, t, :], UV[t][:, 0, 0:GC], ACT.Silu).then_inc(silu_done, 1)

                def ht_high(t):
                    act.wait_ge(ht_psum, n + t)
                    act.activation(ht_hi[:, t], UV[t][:, 1, 0:GC], ACT.Copy).then_inc(ht_hi_done, 1)

                def transposed_and_splits():
                    ht_high(0)
                    if g + 2 < NG:
                        split(l, FFN_AT[f] + up_unit(g + 2), i, 3)
                        split(l, FFN_AT[f] + up_unit(g + 2) + 1, i, 3)
                    split(l, FFN_AT[f] + down_unit(g + 1), i, 3)
                    if g + 2 == NG and f == 0:
                        split(l, MIX_AT)
                    elif g + 2 == NG:
                        split(l, NEXT_UNIT)
                    ht_high(1)

                if g == NG - 1:
                    return silu_block, ht_high
                if g == 0:
                    return silu_block, transposed_and_splits
                silu_block(0)
                silu_block(1)
                transposed_and_splits()

            def ffn(l, f):
                k = 3 * f
                if f == 1:
                    norm_squares(l, k, 0)
                norm_hi(l, k, 0)
                split(l, FFN_AT[f] + 1)
                norm_squares(l, k, 1)
                silu_block, after = ffn_group(l, f, 0)
                silu_block(0)
                norm_hi(l, k, 1)
                split(l, FFN_AT[f] + 2)
                split(l, FFN_AT[f] + 3)
                silu_block(1)
                split(l, FFN_AT[f] + down_unit(0))
                after()
                with act.Fori(0, NG - 3, 2) as i:
                    ffn_group(l, f, 1, i)
                    ffn_group(l, f, 2, i)
                ffn_group(l, f, NG - 2)

            def latent_and_window(l, t):
                act.wait_ge(proj_done, l * TB + (t + 1))
                if t == 1:
                    act.wait_ge(latent_ready, l * TB + t)
                    act.wait_ge(swa_used, l * TB + t)
                act.activation(latent, A[t][:, 0, 0:QR + KVR], ACT.Copy)
                act.activation(swa_raw[:, 512:640], A[t][:, 0, QR + KVR:512], ACT.Copy)
                act.activation(swa_raw[:, 0:512], A[t][:, 1, :], ACT.Copy)
                act.activation(v_swa[:, t, :], UV[t][:, 0, 0:128], ACT.Copy)
                act.activation(kpe[:, t, :], UV[t][:, 0, 128:192], ACT.Copy)
                act.drain()
                act.activation(work[:, 1, 128:128 + QR], latent[:, 0:QR], ACT.Square,
                               scale=QR ** -0.5, accum_out=ss_c[:, t, 0:1])
                act.activation(work[:, 1, 384:384 + KVR], latent[:, QR:], ACT.Square,
                               scale=KVR ** -0.5, accum_out=ss_c[:, t, 1:2]).then_inc(latent_ss, 1)
                act.activation(work[:, 3, 384:448], kpe[:, t, :], ACT.Square, scale=MLA_QK ** -0.5,
                               accum_out=ss_pe[:, t, :])
                act.activation(work[:].rearrange("p a b -> p (a b)")[:, 0:640], swa_raw, ACT.Square,
                               scale=SD ** -0.5).then_inc(swa_copied, 1)

            def latent_high(l, t):
                act.wait_ge(latent_psum, l * TB + (t + 1))
                act.activation(act_hi[:, t, 0:3, :], UV[t][:, 1, 0:384], ACT.Copy).then_inc(latent_hi_done, 1)

            def mla_parts(l, t):
                act.wait_ge(mla_done, l * TB + (t + 1))
                parts = [(UV[t][:, 0, :], NOPE), (A[t][:, 0, :], NOPE), (UV[t][:, 1, 0:256], ROPE)]
                for p, (src, width) in enumerate(parts):
                    for hd in range(MH):
                        c = p * MH + hd
                        at = p * 512 + hd * width
                        act.activation(squares[:, at:at + width], src[:, hd * width:(hd + 1) * width], ACT.Square,
                                       scale=MLA_QK ** -0.5, accum_out=ss_part[:, t, c:c + 1])
                act.activation(v_mla[:, t, :], A[t][:, 1, :], ACT.Copy).then_inc(mla_squares, 1)

            def qk_copies(l, t):
                n = l * (5 * TB) + 5 * t
                act.wait_ge(qk_psum, n + 1)
                act.activation(qt[:, t, 0:4, :], A[t][:, 0, :], ACT.Copy, scale=cgain[:, 0:1]).then_inc(qk_act, 1)
                act.wait_ge(qk_psum, n + 3)
                act.activation(kt[:, 2:6, t, :], heads(UV[t][:, 0, :], 4), ACT.Copy, scale=cgain[:, 1:2])
                act.wait_ge(qk_psum, n + 5)
                act.activation(kt[:, 6, t, :], A[t][:, 0, 0:P], ACT.Copy).then_inc(qk_act, 1)

            def softmax(l, t, b):
                latent_heads, hs = BANKS[t][b]
                wide = (t + 1) * P
                act.wait_ge(shift_ready, bank_no(l, t, b) + 1)
                for j, hd in enumerate(hs):
                    col = hd if latent_heads else MH + hd
                    last = act.activation(probs[:, b % 2, j * wide:(j + 1) * wide],
                                          A[t][:, b % 2, j * wide:(j + 1) * wide], ACT.Exp,
                                          bias=shift[:, b % 2, j:j + 1],
                                          scale=MLA_SCALE if latent_heads else SWA_SCALE,
                                          accum_out=den[:, t, col:col + 1])
                if not latent_heads:
                    last = act.activation(sink_e[:, t, hs[0]:hs[-1] + 1], sink_gap[:, t, hs[0]:hs[-1] + 1],
                                          ACT.Exp)
                last.then_inc(probs_ready, 1)

            def probs_copy(l, t, b):
                w = len(BANKS[t][b][1]) * (t + 1) * P
                act.wait_ge(pt_psum, bank_no(l, t, b) + 1)
                act.activation(probs_t[:, b % 2, 0:w], UV[t][:, 0, 0:w], ACT.Copy).then_inc(pt_ready, 1)

            norm_squares(0, 0, 0)
            split(0, -1)
            with act.Fori(0, DEPTH) as l:
                ffn(l, 0)
                silu_block, ht_high = ffn_group(l, 0, NG - 1)
                silu_block(0)
                ht_high(0)
                silu_block(1)
                split(l, MIX_AT + 1)
                norm_squares(l, 1, 0)
                ht_high(1)
                split(l, MIX_AT + 2)
                norm_hi(l, 1, 0)
                split(l, MIX_AT + 3)
                norm_squares(l, 1, 1)
                split(l, MIX_AT + 4)
                norm_hi(l, 1, 1)
                split(l, MIX_AT + 5)
                act.wait_ge(small_loaded, l * 32 + 32)
                latent_and_window(l, 0)
                latent_high(l, 0)
                mla_parts(l, 0)
                latent_and_window(l, 1)
                act.activation(sink_gap[:, 0, 0:1], consts[:, 0, 0:1], ACT.Exp)
                qk_copies(l, 0)
                latent_high(l, 1)
                softmax(l, 0, 0)
                softmax(l, 0, 1)
                mla_parts(l, 1)
                softmax(l, 0, 2)
                softmax(l, 0, 3)
                probs_copy(l, 0, 2)
                split(l, MIX_AT + 6)
                probs_copy(l, 0, 3)
                norm_squares(l, 2, 0)
                qk_copies(l, 1)
                split(l, MIX_AT + 7)
                softmax(l, 1, 0)
                norm_hi(l, 2, 0)
                probs_copy(l, 1, 0)
                split(l, MIX_AT + 8)
                for b in range(1, len(BANKS[1])):
                    softmax(l, 1, b)
                    probs_copy(l, 1, b)
                    if b == 1:
                        split(l, MIX_AT + 9)
                norm_squares(l, 2, 1)
                norm_hi(l, 2, 1)
                split(l, FFN_AT[1])
                ffn(l, 1)
                silu_block, ht_high = ffn_group(l, 1, NG - 1)
                silu_block(0)
                ht_high(0)
                silu_block(1)
                norm_squares(l, 4, 0)
                ht_high(1)

        @block.vector
        def _(dve):
            def split(l, unit, i=0, di=0):
                for half in range(2):
                    n = half_no(unit, half)
                    dve.wait_ge(hi_done, l * (2 * LU) + i * (2 * di) + (n + 1))
                    dve.tensor_tensor(wlo_half(unit, half), raw[:, n % RAW, :],
                                      whi_half(unit, half).bitcast(F32), ALU.subtract).then_inc(split_done, 1)

            def add_to_x(l, s, t):
                dve.wait_ge(sum_ready, l * 6 + (2 * s + t + 1))
                dve.scalar_tensor_tensor(x[:, t, :], A[t][:].rearrange("p a b -> p (a b)"),
                                         1.0 if s == 1 else 0.5, x[:, t, :], ALU.mult, ALU.add
                                         ).then_inc(x_ready, 1)

            def norm_apply(l, k, t):
                n = 2 * k + t
                if t == 0:
                    dve.wait_ge(gain_loaded[k % 2], l * 32 + 16 * (k // 2 + 1))
                dve.wait_ge(rstd_ready, l * 8 + (n + 1))
                if n:
                    dve.wait_ge(xt_ready, l * 16 + 2 * n)
                for b in range(2):
                    w = slice(b * 512, (b + 1) * 512)
                    src, c = (attn[:, w], b) if k == 2 else (x[:, t, w], 0)
                    dve.scalar_tensor_tensor(xn[:, w], src, rs_x[:, t, c:c + 1], gain[:, k % 2, w], ALU.mult,
                                             ALU.mult).then_inc(xn_ready, 1)

            def norm_lo(l, k, t):
                for b in range(2):
                    dve.wait_ge(act_hi_done, l * 16 + (4 * k + 2 * t + b + 1))
                    dve.tensor_tensor(act_lo[:, t, 4 * b:4 * b + 4, :], heads(UV[t][:, b, :], 4),
                                      act_hi[:, t, 4 * b:4 * b + 4, :].bitcast(F32), ALU.subtract
                                      ).then_inc(act_ready, 1)

            def ffn_group(l, f, g, i=0):
                n = l * (4 * NG) + i * 2 + (2 * (NG * f + g) + 1)

                def gate_times_up(t):
                    dve.wait_ge(silu_done, n + t)
                    dve.tensor_tensor(h[:, t, :], silu[:, t, :], UV[t][:, 0, GC:2 * GC], ALU.mult
                                      ).then_inc(h_ready, 1)

                def ht_low(t):
                    dve.wait_ge(ht_hi_done, n + t)
                    dve.tensor_tensor(ht_lo[:, t], heads(UV[t][:, 1, 0:GC], 2), ht_hi[:, t].bitcast(F32),
                                      ALU.subtract).then_inc(ht_ready, 1)

                def transposed_and_splits():
                    ht_low(0)
                    if g + 2 < NG:
                        split(l, FFN_AT[f] + up_unit(g + 2), i, 3)
                        split(l, FFN_AT[f] + up_unit(g + 2) + 1, i, 3)
                    split(l, FFN_AT[f] + down_unit(g + 1), i, 3)
                    if g + 2 == NG and f == 0:
                        split(l, MIX_AT)
                    elif g + 2 == NG:
                        split(l, NEXT_UNIT)
                    ht_low(1)

                if g == NG - 1:
                    return gate_times_up, ht_low
                if g == 0:
                    return gate_times_up, transposed_and_splits
                gate_times_up(0)
                gate_times_up(1)
                transposed_and_splits()

            def ffn(l, f):
                k = 3 * f
                norm_lo(l, k, 0)
                if f == 1:
                    add_to_x(l, 1, 1)
                split(l, FFN_AT[f] + 1)
                norm_apply(l, k, 1)
                gate_times_up, after = ffn_group(l, f, 0)
                gate_times_up(0)
                norm_lo(l, k, 1)
                split(l, FFN_AT[f] + 2)
                split(l, FFN_AT[f] + 3)
                gate_times_up(1)
                split(l, FFN_AT[f] + down_unit(0))
                after()
                with dve.Fori(0, NG - 3, 2) as i:
                    ffn_group(l, f, 1, i)
                    ffn_group(l, f, 2, i)
                ffn_group(l, f, NG - 2)

            def rotate(src, first, n, t, ready):
                dst = heads(qkn[:, first:first + n // 2, :].rearrange("p a b -> p (a b)"), n)
                src, tmp = heads(src, n), heads(rot_tmp[:, 0:n * ROPE], n)
                hf = ROPE // 2
                dve.tensor_tensor(dst, src, over_heads(cs[:, t, 0, :], n), ALU.mult)
                dve.tensor_tensor(tmp[:, :, 0:hf], src[:, :, hf:ROPE], over_heads(cs[:, t, 1, 0:hf], n), ALU.mult)
                dve.tensor_tensor(tmp[:, :, hf:ROPE], src[:, :, 0:hf], over_heads(cs[:, t, 1, hf:ROPE], n),
                                  ALU.mult)
                dve.drain()
                last = dve.tensor_tensor(dst, dst, tmp, ALU.add)
                if ready:
                    last.then_inc(qkn_ready, 1)

            def latent_norm(l, t):
                dve.wait_ge(latent_rstd, l * TB + (t + 1))
                dve.wait_ge(xt_ready, l * 16 + 8)
                dve.scalar_tensor_tensor(xn[:, 0:QR], latent[:, 0:QR], rs_c[:, t, 0:1],
                                         sgain[:, SG_QA:SG_QA + QR], ALU.mult, ALU.mult)
                dve.scalar_tensor_tensor(xn[:, QR:QR + KVR], latent[:, QR:], rs_c[:, t, 1:2],
                                         sgain[:, SG_KVA:SG_KVA + KVR], ALU.mult, ALU.mult
                                         ).then_inc(latent_ready, 1)

            def window_sums(l, t):
                dve.wait_ge(swa_copied, l * TB + (t + 1))
                flat = work[:].rearrange("p a b -> p (a b)")
                dve.reduce_sum(ss_s[:, t, :], heads(flat[:, 0:640], 10), axis=AX_X).then_inc(swa_ss, 1)

            def window_norm(l, t):
                dve.wait_ge(swa_rstd, l * TB + (t + 1))
                dve.tensor_tensor(heads(rot_in, 10), heads(swa_raw, 10), spread(rs_s[:, t, :], SD), ALU.mult
                                  ).then_inc(swa_used, 1)
                dve.drain()
                q, k = heads(rot_in[:, 0:512], SH), heads(rot_in[:, 512:640], SKV)
                dve.tensor_tensor(q, q, over_heads(sgain[:, SG_SQ:SG_SQ + SD], SH), ALU.mult)
                dve.tensor_tensor(k, k, over_heads(sgain[:, SG_SK:SG_SK + SD], SKV), ALU.mult)
                dve.drain()
                if t == 1:
                    dve.wait_ge(qk_psum, l * (5 * TB) + 5)
                rotate(rot_in, CSQ, 10, t, False)

            def latent_lo(l, t):
                dve.wait_ge(latent_hi_done, l * TB + (t + 1))
                dve.tensor_tensor(act_lo[:, t, 0:3, :], heads(UV[t][:, 1, 0:384], 3),
                                  act_hi[:, t, 0:3, :].bitcast(F32), ALU.subtract).then_inc(latent_act, 1)

            def mla_sums(l, t):
                dve.wait_ge(mla_squares, l * TB + (t + 1))
                dve.tensor_tensor(ss_m[:, t, 0:4], ss_part[:, t, 0:4], ss_part[:, t, 8:12], ALU.add)
                dve.tensor_scalar(ss_m[:, t, 4:8], ss_part[:, t, 4:8], ss_pe[:, t, :], None, ALU.add
                                  ).then_inc(mla_ss, 1)
                dve.tensor_tensor(kpe_g[:], kpe[:, t, :], sgain[:, SG_MK:SG_MK + ROPE], ALU.mult)
                dve.drain()

            def mla_norm(l, t):
                dve.wait_ge(mla_rstd, l * TB + (t + 1))
                q, k = heads(rot_in[:, 0:256], MH), heads(rot_in[:, 256:512], MH)
                dve.tensor_tensor(q, heads(UV[t][:, 1, 0:256], MH), spread(rs_m[:, t, 0:4], ROPE), ALU.mult)
                dve.tensor_tensor(k, over_heads(kpe_g[:], MH), spread(rs_m[:, t, 4:8], ROPE), ALU.mult)
                dve.drain()
                dve.tensor_tensor(q, q, over_heads(sgain[:, SG_MQ:SG_MQ + ROPE], MH), ALU.mult)
                dve.tensor_tensor(qkn[:, CQN:CQN + 4, :], heads(UV[t][:, 0, :], MH), spread(rs_m[:, t, 0:4], NOPE),
                                  ALU.mult)
                dve.tensor_tensor(qkn[:, CKN:CKN + 4, :], heads(A[t][:, 0, :], MH), spread(rs_m[:, t, 4:8], NOPE),
                                  ALU.mult)
                dve.drain()
                rotate(rot_in[:, 0:512], CQR, 8, t, True)

            def qk_copies(l, t):
                n = l * (5 * TB) + 5 * t
                dve.wait_ge(qk_psum, n + 2)
                dve.tensor_copy(qt[:, t, 4:6, :], heads(A[t][:, 1, 0:256], 2))
                dve.tensor_copy(kt[:, 0:2, t, :], heads(A[t][:, 1, 256:512], 2))
                dve.wait_ge(qk_psum, n + 4)
                dve.tensor_copy(qt[:, t, 6:10, :], heads(UV[t][:, 1, :], 4)).then_inc(qk_dve, 1)

            def probs_copy(l, t, b):
                w = len(BANKS[t][b][1]) * (t + 1) * P
                dve.wait_ge(pt_psum, bank_no(l, t, b) + 1)
                dve.tensor_copy(probs_t[:, b % 2, 0:w], UV[t][:, 0, 0:w]).then_inc(pt_ready, 1)

            def maxima(l, t, b):
                latent_heads, hs = BANKS[t][b]
                n, c = bank_no(l, t, b), len(hs)
                dve.wait_ge(scores_done, n + 1)
                dve.reduce_max(maxi[:, b % 2, 0:c], heads(A[t][:, b % 2, 0:c * (t + 1) * P], c), axis=AX_X)
                dve.drain()
                if latent_heads:
                    dve.tensor_scalar(shift[:, b % 2, 0:c], maxi[:, b % 2, 0:c], -MLA_SCALE, None, ALU.mult
                                      ).then_inc(shift_ready, 1)
                    return
                sink = sgain[:, SG_SINK + hs[0]:SG_SINK + hs[0] + c]
                dve.scalar_tensor_tensor(top[:, b % 2, 0:c], maxi[:, b % 2, 0:c], SWA_SCALE, sink, ALU.mult,
                                         ALU.max)
                dve.drain()
                dve.tensor_tensor(sink_gap[:, t, hs[0]:hs[0] + c], sink, top[:, b % 2, 0:c], ALU.subtract)
                dve.tensor_scalar(shift[:, b % 2, 0:c], top[:, b % 2, 0:c], -1.0, None, ALU.mult
                                  ).then_inc(shift_ready, 1)

            def latent_result(l, t):
                dve.wait_ge(pv_done, bank_no(l, t, 1) + 1)
                dve.reciprocal(rden[:, t, 0:MH], den[:, t, 0:MH])
                dve.drain()
                dve.tensor_tensor(heads(attn[:, 0:512], MH), heads(UV[t][:, 1, :], MH),
                                  spread(rden[:, t, 0:MH], MV), ALU.mult).then_inc(attn_ready, 1)

            def window_result(l, t):
                dve.wait_ge(pv_done, bank_no(l, t, len(BANKS[t]) - 1) + 1)
                dve.tensor_tensor(rden[:, t, MH:], den[:, t, MH:], sink_e[:, t, :], ALU.add)
                dve.drain()
                dve.reciprocal(rden[:, t, MH:], rden[:, t, MH:])
                dve.drain()
                dve.tensor_tensor(heads(attn[:, 512:], SH), heads(UV[t][:, 1, :], SH),
                                  spread(rden[:, t, MH:], SD), ALU.mult).then_inc(attn_ready, 1)

            dve.memset(top[:], 0.0).then_inc(split_done, RAW)
            dve.wait_ge(x_loaded[0], 16)
            dve.memset(maxi[:], 0.0).then_inc(x_ready, 1)
            norm_apply(0, 0, 0)
            dve.wait_ge(x_loaded[1], 16)
            dve.memset(shift[:], 0.0).then_inc(x_ready, 1)
            split(0, -1)
            with dve.Fori(0, DEPTH) as l:
                ffn(l, 0)
                gate_times_up, ht_low = ffn_group(l, 0, NG - 1)
                gate_times_up(0)
                ht_low(0)
                gate_times_up(1)
                add_to_x(l, 0, 0)
                split(l, MIX_AT + 1)
                ht_low(1)
                norm_apply(l, 1, 0)
                split(l, MIX_AT + 2)
                norm_lo(l, 1, 0)
                add_to_x(l, 0, 1)
                split(l, MIX_AT + 3)
                norm_apply(l, 1, 1)
                norm_lo(l, 1, 1)
                split(l, MIX_AT + 4)
                split(l, MIX_AT + 5)
                dve.wait_ge(small_loaded, l * 32 + 32)
                dve.wait_ge(rope_loaded, 16)
                latent_norm(l, 0)
                latent_lo(l, 0)
                window_sums(l, 0)
                window_norm(l, 0)
                mla_sums(l, 0)
                mla_norm(l, 0)
                latent_norm(l, 1)
                qk_copies(l, 0)
                latent_lo(l, 1)
                window_sums(l, 1)
                maxima(l, 0, 0)
                maxima(l, 0, 1)
                window_norm(l, 1)
                probs_copy(l, 0, 0)
                maxima(l, 0, 2)
                mla_sums(l, 1)
                probs_copy(l, 0, 1)
                maxima(l, 0, 3)
                latent_result(l, 0)
                mla_norm(l, 1)
                window_result(l, 0)
                split(l, MIX_AT + 6)
                norm_apply(l, 2, 0)
                qk_copies(l, 1)
                split(l, MIX_AT + 7)
                maxima(l, 1, 0)
                maxima(l, 1, 1)
                norm_lo(l, 2, 0)
                split(l, MIX_AT + 8)
                maxima(l, 1, 2)
                split(l, MIX_AT + 9)
                latent_result(l, 1)
                for b in range(3, len(BANKS[1])):
                    maxima(l, 1, b)
                window_result(l, 1)
                norm_apply(l, 2, 1)
                add_to_x(l, 1, 0)
                norm_lo(l, 2, 1)
                norm_apply(l, 3, 0)
                split(l, FFN_AT[1])
                ffn(l, 1)
                gate_times_up, ht_low = ffn_group(l, 1, NG - 1)
                gate_times_up(0)
                ht_low(0)
                gate_times_up(1)
                add_to_x(l, 2, 0)
                ht_low(1)
                norm_apply(l, 4, 0)
                add_to_x(l, 2, 1)

        @block.tensor
        def _(pe):
            def halves_split(l, n, i=0):
                pe.wait_ge(split_done, l * (2 * LU) + i * 6 + (RAW + 2 + n + 1))

            def product(dst, hi, lo, w_hi, w_lo, start, stop):
                pe.matmul(dst, hi, w_hi, start=start, stop=False, skip_group_check=True)
                pe.matmul(dst, hi, w_lo, start=False, stop=False, skip_group_check=True)
                return pe.matmul(dst, lo, w_hi, start=False, stop=stop, skip_group_check=True)

            def transpose_norm(l, k, t):
                for c in range(KD):
                    if c % 4 == 0:
                        pe.wait_ge(xn_ready, l * 16 + (4 * k + 2 * t + c // 4 + 1))
                    last = pe.transpose(UV[t][:, c // 4, (c % 4) * P:(c % 4 + 1) * P], xn[:, c * P:(c + 1) * P],
                                        ident[:])
                    if c % 4 == 3:
                        last.then_inc(xt_ready, 1)
                    elif c == 0 and t == 1 and k != 2:
                        last.then_inc(unit_freed, 1)

            def activations(l, k, t, c):
                if c % 4 == 0:
                    pe.wait_ge(act_ready, l * 16 + (4 * k + 2 * t + c // 4 + 1))

            def up(l, f, g, t, chunks, i=0):
                if g and chunks[0] == 0:
                    pe.wait_ge(h_ready, l * (4 * NG) + i * 2 + (2 * (NG * f + g - 1) + t + 1))
                unit = FFN_AT[f] + up_unit(g)
                for k in chunks:
                    if g == 0:
                        activations(l, 3 * f, t, k)
                    if t == 0 and k % 2 == 0:
                        halves_split(l, 2 * unit + k // 2, i)
                    w = slice((k % 2) * 512, (k % 2 + 1) * 512)
                    u, hf = unit + k // 4, k // 2 % 2
                    last = product(UV[t][:, 0, :], act_hi[:, t, k, :], act_lo[:, t, k, :],
                                   whi_half(u, hf)[:, w], wlo_half(u, hf)[:, w], k == 0, k == KD - 1)
                if chunks[-1] == KD - 1:
                    last.then_inc(up_done, 1)
                return last

            def transpose_h(l, f, g, t, i=0):
                n = l * (4 * NG) + i * 2 + (2 * (NG * f + g) + t + 1)
                pe.wait_ge(h_ready, n)
                for c in range(2):
                    last = pe.transpose(UV[t][:, 1, c * P:(c + 1) * P], h[:, t, c * P:(c + 1) * P], ident[:])
                last.then_inc(ht_psum, 1)

            def down(l, f, g, t, c, i=0):
                unit = FFN_AT[f] + down_unit(g)
                if c == 0:
                    pe.wait_ge(ht_ready, l * (4 * NG) + i * 2 + (2 * (NG * f + g) + t + 1))
                if t == 0:
                    halves_split(l, 2 * unit + c, i)
                for n in range(2):
                    w = slice(n * 512, (n + 1) * 512)
                    last = product(A[t][:, n, :], ht_hi[:, t, c, :], ht_lo[:, t, c, :],
                                   whi_half(unit, c)[:, w], wlo_half(unit, c)[:, w],
                                   g == 0 and c == 0, g == NG - 1 and c == 1)
                return last

            def ffn_step(l, f, g, i=0):
                for t in range(TB):
                    last = up(l, f, g, t, range(0, 4), i)
                    if g == 1 and t == 0:
                        last.then_inc(unit_freed, 2)
                    transpose_h(l, f, g - 1, t, i)
                    up(l, f, g, t, range(4, KD), i)
                    up_freed = down(l, f, g - 1, t, 0, i)
                    down_freed = down(l, f, g - 1, t, 1, i)
                up_freed.then_inc(unit_freed, 2)
                down_freed.then_inc(unit_freed, 1)

            def ffn(l, f):
                up(l, f, 0, 0, range(KD))
                transpose_norm(l, 3 * f, 1)
                up(l, f, 0, 1, range(KD))
                ffn_step(l, f, 1)
                with pe.Fori(0, NG - 3, 2) as i:
                    ffn_step(l, f, 2, i)
                    ffn_step(l, f, 3, i)
                g = NG - 1
                up(l, f, g, 0, range(0, 4))
                transpose_h(l, f, g - 1, 0)
                up(l, f, g, 0, range(4, KD))
                down(l, f, g - 1, 0, 0)
                down(l, f, g - 1, 0, 1)
                up(l, f, g, 1, range(0, 4))
                transpose_h(l, f, g - 1, 1)
                up(l, f, g, 1, range(4, 6))
                transpose_h(l, f, g, 0)
                up(l, f, g, 1, range(6, KD))
                down(l, f, g, 0, 0).then_inc(unit_freed, 2)
                down(l, f, g, 0, 1).then_inc(sum_ready, 1)
                down(l, f, g - 1, 1, 0)
                down(l, f, g - 1, 1, 1).then_inc(unit_freed, 1)
                transpose_h(l, f, g, 1)
                down(l, f, g, 1, 0)
                transpose_norm(l, 1 if f == 0 else 4, 0)
                down(l, f, g, 1, 1).then_inc(sum_ready, 1)

            def input_main(l, t, chunks):
                for k in chunks:
                    u, hf = MIX_AT + k // 2, k % 2
                    activations(l, 1, t, k)
                    if t == 0:
                        halves_split(l, 2 * u + hf)
                    for n in range(2):
                        w = slice(n * 512, (n + 1) * 512)
                        last = product(A[t][:, n, :], act_hi[:, t, k, :], act_lo[:, t, k, :],
                                       whi_half(u, hf)[:, w], wlo_half(u, hf)[:, w], k == 0, k == KD - 1)
                return last

            def input_tail(l, t):
                for k in range(KD):
                    u, hf = MIX_AT + 4, k // 4
                    if t == 0 and k % 4 == 0:
                        halves_split(l, 2 * u + hf)
                    w = slice((k % 4) * 192, (k % 4 + 1) * 192)
                    last = product(UV[t][:, 0, 0:192], act_hi[:, t, k, :], act_lo[:, t, k, :],
                                   whi_half(u, hf)[:, w], wlo_half(u, hf)[:, w], k == 0, k == KD - 1)
                return last.then_inc(proj_done, 1)

            def transpose_latent(l, t):
                pe.wait_ge(latent_ready, l * TB + (t + 1))
                for c in range(3):
                    last = pe.transpose(UV[t][:, 1, c * P:(c + 1) * P], xn[:, c * P:(c + 1) * P], ident[:])
                last.then_inc(latent_psum, 1)

            def latent_products(l, t):
                pe.wait_ge(latent_act, l * TB + (t + 1))
                u = MIX_AT + 5
                if t == 0:
                    halves_split(l, 2 * u + 1)
                for n in range(2):
                    w = slice(n * 512, (n + 1) * 512)
                    product(A[t][:, n, :], act_hi[:, t, 2, :], act_lo[:, t, 2, :],
                            whi_half(u, 1)[:, w], wlo_half(u, 1)[:, w], True, True)
                for k in range(2):
                    w = slice(k * 512, (k + 1) * 512)
                    product(UV[t][:, 0, :], act_hi[:, t, k, :], act_lo[:, t, k, :],
                            whi_half(u, 0)[:, w], wlo_half(u, 0)[:, w], k == 0, k == 1)
                for k in range(2):
                    w = slice(768, 1024)
                    last = product(UV[t][:, 1, 0:256], act_hi[:, t, k, :], act_lo[:, t, k, :],
                                   whi_half(u - 1, k)[:, w], wlo_half(u - 1, k)[:, w], k == 0, k == 1)
                return last.then_inc(mla_done, 1)

            def transpose_qk(l, t):
                n = l * (5 * TB) + 5 * t
                pe.wait_ge(qkn_ready, l * TB + (t + 1))
                banks = [A[t][:, 0, :], A[t][:, 1, :], UV[t][:, 0, :], UV[t][:, 1, :], A[t][:, 0, :]]
                for b, bank in enumerate(banks):
                    if b == 4:
                        pe.wait_ge(qk_act, l * (2 * TB) + (2 * t + 1))
                    for c in range(4 * b, min(4 * b + 4, CHUNKS)):
                        last = pe.transpose(bank[:, (c % 4) * P:(c % 4 + 1) * P], qkn[:, c, :], ident[:])
                    last.then_inc(qk_psum, 1)

            def scores(l, t, b):
                latent_heads, hs = BANKS[t][b]
                n, wide = bank_no(l, t, b), (t + 1) * P
                if b >= 2:
                    pe.wait_ge(probs_ready, n - 1)
                for j, hd in enumerate(hs):
                    dst = A[t][:, b % 2, j * wide:(j + 1) * wide]
                    if latent_heads:
                        r = ROPE * (hd % 2)
                        pe.matmul(dst, qt[:, t, hd, :], kt[:, 2 + hd, 0:t + 1, :], start=True, stop=False,
                                  skip_group_check=True)
                        pe.matmul(dst, qt[r:r + ROPE, t, 4 + hd // 2, :], kt[r:r + ROPE, hd // 2, 0:t + 1, :],
                                  start=False, stop=False, skip_group_check=True)
                        last = pe.matmul(dst[:, t * P:wide], ident_b[:], masks[:, 1, :], start=False, stop=True,
                                         skip_group_check=True)
                    else:
                        r = SD * (hd // 4)
                        pe.matmul(dst, qt[r:r + SD, t, 6 + hd % 4, :], kt[r:r + SD, 6, 0:t + 1, :], start=True,
                                  stop=False, skip_group_check=True)
                        last = pe.matmul(dst, ident_b[:], masks[:, 1 - t:2, :], start=False, stop=True,
                                         skip_group_check=True)
                    first = last if j == 0 else first
                last.then_inc(scores_done, 1)
                return first

            def transpose_probs(l, t, b):
                pe.wait_ge(probs_ready, bank_no(l, t, b) + 1)
                if b:
                    pe.wait_ge(pt_ready, bank_no(l, t, b))
                for c in range(len(BANKS[t][b][1]) * (t + 1)):
                    last = pe.transpose(UV[t][:, 0, c * P:(c + 1) * P], probs[:, b % 2, c * P:(c + 1) * P], ident[:])
                last.then_inc(pt_psum, 1)

            def values(l, t, b):
                latent_heads, hs = BANKS[t][b]
                n = bank_no(l, t, b)
                pe.wait_ge(pt_ready, n + 1)
                if not latent_heads and hs[0] == 0:
                    pe.wait_ge(attn_ready, l * 4 + (2 * t + 1))
                for j, hd in enumerate(hs):
                    for c in range(t + 1):
                        if latent_heads:
                            dst, v = UV[t][:, 1, hd * MV:(hd + 1) * MV], v_mla[:, c, hd * MV:(hd + 1) * MV]
                        else:
                            kv = hd // (SH // SKV)
                            dst, v = UV[t][:, 1, hd * SD:(hd + 1) * SD], v_swa[:, c, kv * SD:(kv + 1) * SD]
                        last = pe.matmul(dst, probs_t[:, b % 2, (j * (t + 1) + c) * P:(j * (t + 1) + c + 1) * P], v,
                                         start=c == 0, stop=c == t, skip_group_check=True)
                last.then_inc(pv_done, 1)

            def output_chunk(l, t, k):
                u, hf = MIX_AT + 6 + k // 2, k % 2
                activations(l, 2, t, k)
                if t == 0:
                    halves_split(l, 2 * u + hf)
                for n in range(2):
                    w = slice(n * 512, (n + 1) * 512)
                    last = product(A[t][:, n, :], act_hi[:, t, k, :], act_lo[:, t, k, :],
                                   whi_half(u, hf)[:, w], wlo_half(u, hf)[:, w], k == 0, k == KD - 1)
                if k == KD - 1:
                    last.then_inc(sum_ready, 1)
                elif k % 2 and t == 1:
                    last.then_inc(unit_freed, 1)

            pe.wait_ge(const_ready, 1)
            transpose_norm(0, 0, 0)
            with pe.Fori(0, DEPTH) as l:
                ffn(l, 0)
                input_main(l, 0, range(0, 4))
                transpose_norm(l, 1, 1)
                input_main(l, 0, range(4, KD))
                input_tail(l, 0)
                input_main(l, 1, range(0, 3))
                transpose_latent(l, 0)
                input_main(l, 1, range(3, 5))
                latent_products(l, 0)
                input_main(l, 1, range(5, KD)).then_inc(unit_freed, 4)
                input_tail(l, 1)
                transpose_qk(l, 0)
                transpose_latent(l, 1)
                pe.wait_ge(qk_act, l * (2 * TB) + 2)
                pe.wait_ge(qk_dve, l * TB + 1)
                scores(l, 0, 0)
                scores(l, 0, 1)
                latent_products(l, 1)
                transpose_probs(l, 0, 0)
                scores(l, 0, 2).then_inc(unit_freed, 2)
                values(l, 0, 0)
                transpose_probs(l, 0, 1)
                scores(l, 0, 3)
                values(l, 0, 1)
                transpose_probs(l, 0, 2)
                values(l, 0, 2)
                transpose_probs(l, 0, 3)
                values(l, 0, 3)
                transpose_qk(l, 1)
                pe.wait_ge(qk_act, l * (2 * TB) + 4)
                pe.wait_ge(qk_dve, l * TB + 2)
                scores(l, 1, 0)
                scores(l, 1, 1)
                transpose_norm(l, 2, 0)
                for b in range(KD):
                    if b < len(BANKS[1]):
                        transpose_probs(l, 1, b)
                    output_chunk(l, 0, b)
                    if b < len(BANKS[1]):
                        values(l, 1, b)
                    if b + 2 < len(BANKS[1]):
                        scores(l, 1, b + 2)
                transpose_norm(l, 2, 1)
                for b in range(KD):
                    output_chunk(l, 1, b)
                    if b == 5:
                        transpose_norm(l, 3, 0)
                ffn(l, 1)


def kernel(**inputs):
    import numpy as np
    import concourse.bacc as bacc
    from concourse.bass_utils import run_bass_kernel_spmd as run

    a = {n: np.ascontiguousarray(v) for n, v in inputs.items()}

    def halves(l):
        out = []

        def up(f, g):
            w = [a[f"ffn{f + 1}_w_{n}"][l][:, g * GC:(g + 1) * GC].reshape(KD // 2, 2, P, GC)
                 for n in ("gate", "up")]
            out.extend(np.stack(w, 3).transpose(0, 2, 1, 3, 4).reshape(KD // 2, P, HC))

        def down(f, g):
            out.extend(a[f"ffn{f + 1}_w_down"][l][g * GC:(g + 1) * GC].reshape(2, P, HC))

        def ffn(f):
            up(f, 0)
            up(f, 1)
            for g in range(NG):
                down(f, g)
                if g + 2 < NG:
                    up(f, g + 2)

        ffn(0)
        w = a["w_in"][l]
        at = np.cumsum([0, QR, KVR, ROPE, SH * SD, SKV * SD, SKV * SD])
        cq, ckv, kpe, qs, ks, vs = (w[:, at[j]:at[j + 1]] for j in range(6))
        qs = qs.reshape(D, SKV, SH // SKV, SD).transpose(0, 2, 1, 3).reshape(D, SH * SD)
        out.extend(np.concatenate([cq, ckv, ks, qs], 1).reshape(KD, P, HC))
        tail = np.concatenate([vs, kpe], 1).reshape(2, 4, P, 192).transpose(0, 2, 1, 3).reshape(2, P, 768)
        qb = a["mla_w_q_b"][l].reshape(2, P, MH, MLA_QK)
        q_nope, q_rope = qb[..., :NOPE].reshape(2, P, 512), qb[..., NOPE:].reshape(2, P, 256)
        out.extend(np.concatenate([tail, q_rope], 2))
        out.append(q_nope.transpose(1, 0, 2).reshape(P, HC))
        out.append(a["mla_w_kv_b"][l].reshape(P, MH, 2, P).transpose(0, 2, 1, 3).reshape(P, HC))
        out.extend(a["w_o"][l].reshape(KD, P, HC))
        ffn(1)
        return out

    f32 = np.float32
    stream = np.stack([t for l in range(DEPTH) for t in halves(l)])
    norm_gains = np.stack([g for l in range(DEPTH) for g in (
        a["ffn1_norm"][l], a["mix_norm"][l], np.concatenate([a["mla_out_norm"][l], a["swa_out_norm"][l]]),
        a["ffn2_norm"][l])] + [a["ffn1_norm"][0]])
    small = np.concatenate([a["mla_q_a_norm"], a["mla_kv_a_norm"], a["swa_q_norm"], a["swa_k_norm"],
                            a["mla_q_norm"][:, NOPE:], a["mla_k_norm"][:, NOPE:], a["swa_sinks"]], 1)
    cols = np.ascontiguousarray(np.stack([a["mla_q_norm"][:, :NOPE], a["mla_k_norm"][:, :NOPE]], 2))
    inv = 1.0 / (f32(10000.0) ** (np.arange(0, ROPE, 2, dtype=f32) / f32(ROPE)))
    angle = np.arange(SEQ, dtype=f32)[:, None] * inv[None, :].astype(f32)
    c, s = np.cos(angle).astype(f32), np.sin(angle).astype(f32)
    rope = np.stack([np.concatenate([c, c], 1), np.concatenate([-s, s], 1)], 1).reshape(TB, P, 2, ROPE)

    arrays = {"x_in": a["x"].reshape(SEQ, D), "stream": stream, "norm_gains": norm_gains, "small_gains": small,
              "col_gains": cols, "rope": np.ascontiguousarray(rope)}
    nc = bacc.Bacc("TRN2", target_bir_lowering=False, num_devices=1)
    args = [nc.dram_tensor(n, v.shape, F32, kind="ExternalInput").ap() for n, v in arrays.items()]
    result = nc.dram_tensor("out", (SEQ, D), F32, kind="ExternalOutput").ap()
    hybrid_trunk(nc, *args, result)
    r = run(nc, [arrays], core_ids=[0])
    return r.results[0]["out"].reshape(1, SEQ, D)
```

```python
from contextlib import ExitStack

import concourse.bass as bass
from concourse import mybir

ALU = mybir.AluOpType
ACT = mybir.ActivationFunctionType
AX_X = mybir.AxisListType.X
F32 = mybir.dt.float32
F32R = mybir.dt.float32r
BF16 = mybir.dt.bfloat16

P = 128
D = 1024
SEQ = 256
DEPTH = 2
TB = SEQ // P
KD = D // P
EPS = 1e-6
FF = 2816
GC = 256
NG = FF // GC
QR, KVR = 256, 128
MH, NOPE, ROPE, MV = 4, 128, 64, 128
SH, SKV, SD = 8, 2, 64
MLA_QK = NOPE + ROPE
MLA_SCALE = MLA_QK ** -0.5
SWA_SCALE = SD ** -0.5
MASKED = -1e30

RAW = 4
UNITS = 6
HC = 1024
FFN_UNITS = 3 * NG
MIX_UNITS = 10
LU = 2 * FFN_UNITS + MIX_UNITS
FFN_AT = (-1, FFN_UNITS - 1 + MIX_UNITS)
MIX_AT = FFN_UNITS - 1
NEXT_UNIT = LU - 1
NORMS = 4

SG_QA, SG_KVA = 0, QR
SG_SQ = QR + KVR
SG_SK, SG_MQ, SG_MK, SG_SINK = SG_SQ + 64, SG_SQ + 128, SG_SQ + 192, SG_SQ + 256
SG = SG_SINK + SH

CQN, CQR, CKR, CKN, CSQ, CSK, CHUNKS = 0, 4, 6, 8, 12, 16, 17


def half_no(unit, half):
    return 2 * (unit + 1) + half


def up_unit(g):
    return 2 * g if g < 2 else 3 * g - 1


def down_unit(g):
    return 4 + 3 * g if g < NG - 1 else FFN_UNITS - 1


def unit_slots():
    def ffn(first):
        slots = [None] * FFN_UNITS
        for g in range(NG):
            base = (first + 3 * g) % UNITS
            slots[up_unit(g)], slots[up_unit(g) + 1], slots[down_unit(g)] = base, base + 1, base + 2
        return slots

    slots = ffn(0) + [3, 4, 0, 1, 5, 2, 3, 4, 0, 1] + ffn(3)
    twice = slots + slots
    back = {}
    for u in range(LU, 2 * LU):
        last = max(v for v in range(u) if twice[v] == twice[u])
        back[u - LU - 1] = min(u - last, UNITS)
    slot = {u - 1: slots[u] for u in range(LU)}
    slot[NEXT_UNIT], back[NEXT_UNIT] = slot[-1], back[-1]
    return slot, back


SLOT, BACK = unit_slots()


def hybrid_trunk(nc, x_in, stream, norm_gains, small_gains, col_gains, rope, out):
    with ExitStack() as ctx:
        def sb(name, shape, dt=F32):
            return ctx.enter_context(nc.sbuf_tensor(name, shape, dt))

        def pb(name, shape):
            return ctx.enter_context(nc.psum_tensor(name, shape, F32))

        def sem(name):
            return ctx.enter_context(nc.semaphore(name))

        def heads(ap, n):
            return ap.rearrange("p (n d) -> p n d", n=n)

        raw = sb("raw", [P, RAW, HC])
        whi = sb("whi", [P, UNITS, 2 * HC], F32R)
        wlo = sb("wlo", [P, UNITS, 2 * HC], F32R)
        x = sb("x", [P, TB, D])
        act_hi = sb("act_hi", [P, TB, KD, P], F32R)
        act_lo = sb("act_lo", [P, TB, KD, P], F32R)
        gain = sb("gain", [P, 2, D])
        sgain = sb("sgain", [P, SG])
        cgain = sb("cgain", [P, 2])
        cs = sb("cs", [P, TB, 2, ROPE])
        xn = sb("xn", [P, D])
        rot = sb("rot", [P, 2 * 640])
        rot_in, rot_tmp = rot[:, 0:640], rot[:, 640:1280]
        attn = sb("attn", [P, D])
        swa_raw = xn[:, 384:D]
        ht_hi = sb("ht_hi", [P, TB, 2, P], F32R)
        ht_lo = sb("ht_lo", [P, TB, 2, P], F32R)
        work = sb("work", [P, 4, 512])
        silu = heads(work[:, 0, :], TB)
        h = heads(work[:, 1, :], TB)
        probs = work[:, 0:2, :]
        probs_t = work[:, 2:4, :]
        kpe = sb("kpe", [P, TB, ROPE])
        kpe_g = sb("kpe_g", [P, ROPE])
        qkn = sb("qkn", [P, CHUNKS, P])
        squares = qkn[:].rearrange("p a b -> p (a b)")
        qt = sb("qt", [P, TB, 10, P])
        kt = sb("kt", [P, 7, TB, P])
        v_mla = sb("v_mla", [P, TB, MH * MV])
        v_swa = sb("v_swa", [P, TB, SKV * SD])
        ident = sb("ident", [P, P])
        ident_b = sb("ident_b", [P, P], BF16)
        masks = sb("masks", [P, 2, P], BF16)
        consts = sb("consts", [P, 2, 16])
        ss_x = sb("ss_x", [P, TB, 2])
        rs_x = sb("rs_x", [P, TB, 2])
        ss_c = sb("ss_c", [P, TB, 2])
        rs_c = sb("rs_c", [P, TB, 2])
        ss_s = sb("ss_s", [P, TB, 10])
        rs_s = sb("rs_s", [P, TB, 10])
        ss_part = sb("ss_part", [P, TB, 12])
        ss_pe = sb("ss_pe", [P, TB, 1])
        ss_m = sb("ss_m", [P, TB, 8])
        rs_m = sb("rs_m", [P, TB, 8])
        top = sb("top", [P, 2, 4])
        shift = sb("shift", [P, 2, 4])
        sink_gap = sb("sink_gap", [P, TB, SH])
        sink_e = sb("sink_e", [P, TB, SH])
        den = sb("den", [P, TB, MH + SH])
        rden = sb("rden", [P, TB, MH + SH])
        maxi = sb("maxi", [P, 2, 4])

        UV = [pb(f"UV{t}", [P, 2, 512]) for t in range(TB)]
        A = [pb(f"A{t}", [P, 2, 512]) for t in range(TB)]

        raw_landed = [sem(f"raw_landed{r}") for r in range(RAW)]
        hi_done = sem("hi_done")
        split_done = sem("split_done")
        unit_freed = sem("unit_freed")
        x_loaded = [sem("x_loaded0"), sem("x_loaded1")]
        rope_loaded = sem("rope_loaded")
        gain_loaded = [sem("gain_loaded0"), sem("gain_loaded1")]
        small_loaded = sem("small_loaded")
        const_ready = sem("const_ready")
        pool_step = sem("pool_step")
        x_ready = sem("x_ready")
        ss_ready = sem("ss_ready")
        rstd_ready = sem("rstd_ready")
        xn_ready = sem("xn_ready")
        xt_ready = sem("xt_ready")
        act_hi_done = sem("act_hi_done")
        act_ready = sem("act_ready")
        up_done = sem("up_done")
        silu_done = sem("silu_done")
        h_ready = sem("h_ready")
        ht_psum = sem("ht_psum")
        ht_hi_done = sem("ht_hi_done")
        ht_ready = sem("ht_ready")
        sum_ready = sem("sum_ready")
        main_done = sem("main_done")
        proj_done = sem("proj_done")
        latent_ss = sem("latent_ss")
        latent_rstd = sem("latent_rstd")
        latent_ready = sem("latent_ready")
        latent_psum = sem("latent_psum")
        latent_hi_done = sem("latent_hi_done")
        latent_act = sem("latent_act")
        swa_copied = sem("swa_copied")
        swa_ss = sem("swa_ss")
        swa_rstd = sem("swa_rstd")
        swa_used = sem("swa_used")
        mla_done = sem("mla_done")
        mla_squares = sem("mla_squares")
        mla_ss = sem("mla_ss")
        mla_rstd = sem("mla_rstd")
        qkn_ready = sem("qkn_ready")
        qk_psum = sem("qk_psum")
        qk_act = sem("qk_act")
        qk_dve = sem("qk_dve")
        scores_done = sem("scores_done")
        shift_ready = sem("shift_ready")
        probs_ready = sem("probs_ready")
        pt_psum = sem("pt_psum")
        pt_ready = sem("pt_ready")
        pv_done = sem("pv_done")
        attn_ready = sem("attn_ready")
        stored = sem("stored")

        def ht_at(g, t):
            return 0 if g == NG - 1 else t

        def whi_half(unit, half):
            return whi[:, SLOT[unit], half * HC:(half + 1) * HC]

        def wlo_half(unit, half):
            return wlo[:, SLOT[unit], half * HC:(half + 1) * HC]

        def spread(ap, n):
            return ap.unsqueeze(2).to_broadcast([P, ap.shape[1], n])

        def over_heads(ap, n):
            return ap.unsqueeze(1).to_broadcast([P, n, ap.shape[1]])

        def score_banks(t):
            per = 4 // (t + 1)
            return [(True, [0, 2]), (True, [1, 3])] + [(False, list(range(i, i + per))) for i in range(0, SH, per)]

        BANKS = [score_banks(t) for t in range(TB)]
        LB = len(BANKS[0]) + len(BANKS[1])

        def bank_no(l, t, b):
            return l * LB + (len(BANKS[0]) if t else 0) + b

        block = ctx.enter_context(nc.Block())

        @block.sync
        def _(sp):
            sp.dma_start(x[:, 0, :], x_in[0:P, :]).then_inc(x_loaded[0], 16)
            with sp.Fori(0, DEPTH * LU * 2 // RAW) as i:
                for r in range(RAW):
                    sp.wait_ge(split_done, i * RAW + (r + 1))
                    sp.dma_start(raw[:, r, :], stream[bass.ds(i * RAW + r, 1)].rearrange("a p n -> (a p) n")
                                 ).then_inc(raw_landed[r], 16)
            for r in range(2):
                sp.wait_ge(split_done, DEPTH * LU * 2 + r + 1)
                sp.dma_start(raw[:, r, :], stream[r]).then_inc(raw_landed[r], 16)
            for t in range(TB):
                sp.wait_ge(x_ready, DEPTH * 6 + t + 1)
                sp.dma_start(out[t * P:(t + 1) * P, :], x[:, t, :]).then_inc(stored, 16)
            sp.wait_ge(stored, 16 * TB)

        @block.gpsimd
        def _(pool):
            def load_gain(l, k):
                src = norm_gains[bass.ds(l * NORMS + k, 1), :].to_broadcast([P, D])
                pool.dma_start(gain[:, k % 2, :], src).then_inc(gain_loaded[k % 2], 16)

            load_gain(0, 0)
            pool.memset(consts[:, 1, :], EPS)
            pool.memset(consts[:, 0, :], -0.5).then_inc(unit_freed, UNITS - 1)
            pool.memset(ident[:], 0.0)
            pool.memset(ident_b[:], 0.0)
            pool.memset(masks[:], 0.0).then_inc(pool_step, 1)
            pool.wait_ge(pool_step, 1)
            for m in (ident, ident_b):
                pool.affine_select(out=m[:], in_=m[:], compare_op=ALU.not_equal, fill=1.0, base=0,
                                   pattern=[[-1, P]], channel_multiplier=1)
            pool.affine_select(out=masks[:, 0, :], in_=masks[:, 0, :], compare_op=ALU.is_gt, fill=MASKED,
                               base=0, pattern=[[1, P]], channel_multiplier=-1)
            pool.affine_select(out=masks[:, 1, :], in_=masks[:, 1, :], compare_op=ALU.is_ge, fill=MASKED,
                               base=0, pattern=[[-1, P]], channel_multiplier=1).then_inc(const_ready, 1)

            def rstd(l, rs, ms, ready, n):
                pool.tensor_tensor(rs, ms, consts[:, 1, 0:ms.shape[1]], ALU.add).then_inc(pool_step, 1)
                pool.wait_ge(pool_step, l * 14 + (n + 2))
                pool.tensor_tensor(rs, rs, consts[:, 0, 0:ms.shape[1]], ALU.pow).then_inc(ready, 1)

            def norm_rstd(l, k, t):
                pool.wait_ge(ss_ready, l * 8 + (2 * k + t + 1))
                w = 2 if k == 2 else 1
                rstd(l, rs_x[:, t, 0:w], ss_x[:, t, 0:w], rstd_ready, 2 * k + t + (6 if k > 1 else 0))

            norm_rstd(0, 0, 0)
            pool.dma_start(cs[:], rope.rearrange("t p a d -> p t a d")).then_inc(rope_loaded, 16)
            with pool.Fori(0, DEPTH) as l:
                pool.dma_start(sgain[:], small_gains[bass.ds(l, 1), :].to_broadcast([P, SG])
                               ).then_inc(small_loaded, 16)
                pool.dma_start(cgain[:], col_gains[bass.ds(l, 1)].rearrange("a p c -> (a p) c")
                               ).then_inc(small_loaded, 16)
                load_gain(l, 1)
                norm_rstd(l, 0, 1)
                pool.wait_ge(xn_ready, l * 16 + 4)
                load_gain(l, 2)
                norm_rstd(l, 1, 0)
                norm_rstd(l, 1, 1)
                pool.wait_ge(xn_ready, l * 16 + 8)
                load_gain(l, 3)
                def latent(t):
                    pool.wait_ge(latent_ss, l * TB + (t + 1))
                    rstd(l, rs_c[:, t, :], ss_c[:, t, :], latent_rstd, 4 + 3 * t)

                def window(t):
                    pool.wait_ge(swa_ss, l * TB + (t + 1))
                    rstd(l, rs_s[:, t, :], ss_s[:, t, :], swa_rstd, 5 + 3 * t)

                def mla(t):
                    pool.wait_ge(mla_ss, l * TB + (t + 1))
                    rstd(l, rs_m[:, t, :], ss_m[:, t, :], mla_rstd, 6 + 3 * t)

                for t in range(TB):
                    latent(t)
                    window(t)
                    mla(t)
                for k in (2, 3):
                    for t in range(TB):
                        norm_rstd(l, k, t)
                    if k == 2:
                        pool.wait_ge(xn_ready, l * 16 + 12)
                        load_gain(l, 4)
                norm_rstd(l, 4, 0)

        @block.scalar
        def _(act):
            def split(l, unit, i=0, di=0, part=range(2)):
                for half in part:
                    n = half_no(unit, half)
                    act.wait_ge(raw_landed[n % RAW], l * (16 * 2 * LU // RAW) + i * (16 * 2 * di // RAW)
                                + 16 * (n // RAW + 1))
                    if half == 0:
                        act.wait_ge(unit_freed, l * LU + i * di + (unit + 1 - BACK[unit] + 1 + UNITS))
                    act.activation(whi_half(unit, half), raw[:, n % RAW, :], ACT.Copy).then_inc(hi_done, 1)

            def attn_squares(l, t, seg):
                act.wait_ge(attn_ready, l * 4 + (2 * t + seg + 1))
                sq = act.activation(squares[:, seg * 512:(seg + 1) * 512], attn[:, seg * 512:(seg + 1) * 512],
                                    ACT.Square, scale=(D // 2) ** -0.5, accum_out=ss_x[:, t, seg:seg + 1])
                if seg == 1:
                    sq.then_inc(ss_ready, 1)

            def norm_squares(l, k, t):
                if k == 2:
                    for seg in range(2):
                        attn_squares(l, t, seg)
                    return
                act.wait_ge(x_ready, l * 6 + (2 * {0: 0, 1: 1, 3: 2, 4: 3}[k] + t + 1))
                act.activation(UV[t][:].rearrange("p a b -> p (a b)"), x[:, t, :], ACT.Square,
                               scale=D ** -0.5, accum_out=ss_x[:, t, 0:1]).then_inc(ss_ready, 1)

            def norm_hi(l, k, t, banks=range(2)):
                for b in banks:
                    act.wait_ge(xt_ready, l * 16 + (4 * k + 2 * t + b + 1))
                    act.activation(act_hi[:, t, 4 * b:4 * b + 4, :], UV[t][:, b, :], ACT.Copy
                                   ).then_inc(act_hi_done, 1)

            def ffn_group(l, f, g, i=0):
                n = l * (4 * NG) + i * 2 + (2 * (NG * f + g) + 1)

                def silu_block(t):
                    act.wait_ge(up_done, n + t)
                    act.activation(silu[:, t, :], UV[t][:, 0, 0:GC], ACT.Silu).then_inc(silu_done, 1)

                def ht_high(t):
                    act.wait_ge(ht_psum, n + t)
                    act.activation(ht_hi[:, ht_at(g, t)], UV[t][:, 1, 0:GC], ACT.Copy).then_inc(ht_hi_done, 1)

                def transposed_and_splits():
                    ht_high(0)
                    if g + 2 < NG:
                        split(l, FFN_AT[f] + up_unit(g + 2), i, 3)
                        split(l, FFN_AT[f] + up_unit(g + 2) + 1, i, 3)
                    if g == 0:
                        ht_high(1)
                    split(l, FFN_AT[f] + down_unit(g + 1), i, 3)
                    if g + 2 == NG and f == 0:
                        split(l, MIX_AT)
                    elif g + 2 == NG:
                        split(l, NEXT_UNIT)
                    if g:
                        ht_high(1)

                if g == NG - 1:
                    return silu_block, ht_high
                if g == 0:
                    return silu_block, transposed_and_splits
                silu_block(0)
                silu_block(1)
                transposed_and_splits()

            def ffn(l, f):
                k = 3 * f
                split(l, FFN_AT[f] + 1)
                norm_squares(l, k, 1)
                split(l, FFN_AT[f] + 2, part=[0])
                norm_hi(l, k, 1)
                silu_block, after = ffn_group(l, f, 0)
                silu_block(0)
                split(l, FFN_AT[f] + 2, part=[1])
                split(l, FFN_AT[f] + 3)
                silu_block(1)
                split(l, FFN_AT[f] + down_unit(0))
                after()
                with act.Fori(0, NG - 3, 2) as i:
                    ffn_group(l, f, 1, i)
                    ffn_group(l, f, 2, i)
                ffn_group(l, f, NG - 2)

            def latent_and_window(l, t):
                act.wait_ge(main_done, l * TB + (t + 1))
                if t == 1:
                    act.wait_ge(swa_used, l * TB + t)
                act.activation(work[:, 1, 128:128 + QR], A[t][:, 0, 0:QR], ACT.Square,
                               scale=QR ** -0.5, accum_out=ss_c[:, t, 0:1])
                act.activation(work[:, 1, 384:384 + KVR], A[t][:, 0, QR:QR + KVR], ACT.Square,
                               scale=KVR ** -0.5, accum_out=ss_c[:, t, 1:2])
                act.activation(swa_raw[:, 512:640], A[t][:, 0, QR + KVR:512], ACT.Copy)
                flat = work[:].rearrange("p a b -> p (a b)")
                act.activation(flat[:, 512:640], A[t][:, 0, QR + KVR:512], ACT.Square, scale=SD ** -0.5
                               ).then_inc(latent_ss, 1)
                act.activation(swa_raw[:, 0:512], A[t][:, 1, :], ACT.Copy)
                act.activation(flat[:, 0:512], A[t][:, 1, :], ACT.Square, scale=SD ** -0.5
                               ).then_inc(swa_copied, 1)
                act.wait_ge(proj_done, l * TB + (t + 1))
                act.activation(v_swa[:, t, :], UV[t][:, 0, 0:128], ACT.Copy)
                act.activation(kpe[:, t, :], UV[t][:, 0, 128:192], ACT.Copy)
                act.activation(work[:, 3, 384:448], UV[t][:, 0, 128:192], ACT.Square, scale=MLA_QK ** -0.5,
                               accum_out=ss_pe[:, t, :])

            def latent_high(l, t):
                act.wait_ge(latent_psum, l * TB + (t + 1))
                act.activation(act_hi[:, t, 0:3, :], UV[t][:, 1, 0:384], ACT.Copy).then_inc(latent_hi_done, 1)

            def mla_parts(l, t):
                act.wait_ge(mla_done, l * TB + (t + 1))
                for p, src in enumerate([UV[t][:, 0, :], A[t][:, 0, :]]):
                    for c in range(p * MH, (p + 1) * MH):
                        w = slice((c % MH) * NOPE, (c % MH + 1) * NOPE)
                        sq = act.activation(squares[:, c * NOPE:(c + 1) * NOPE], src[:, w], ACT.Square,
                                            scale=MLA_QK ** -0.5, accum_out=ss_part[:, t, c:c + 1])
                        if t == 1 and c == 0:
                            act.activation(v_mla[:, t, :], A[t][:, 1, :], ACT.Copy)
                sq.then_inc(mla_squares, 1)

            def qk_copies(l, t):
                n = l * (5 * TB) + 5 * t
                act.wait_ge(qk_psum, n + 1)
                act.activation(qt[:, t, 0:4, :], A[t][:, 0, :], ACT.Copy, scale=cgain[:, 0:1]).then_inc(qk_act, 1)
                act.wait_ge(qk_psum, n + 2)
                act.activation(kt[:, 2:6, t, :], heads(UV[t][:, 0, :], 4), ACT.Copy, scale=cgain[:, 1:2])
                act.wait_ge(qk_psum, n + 3)
                act.activation(qt[:, t, 6:10, :], heads(UV[t][:, 1, :], 4), ACT.Copy)

            def swa_k_copy(l, t):
                act.wait_ge(qk_psum, l * (5 * TB) + 5 * t + 5)
                act.activation(kt[:, 6, t, :], A[t][:, 0, 0:P], ACT.Copy).then_inc(qk_act, 1)

            def softmax(l, t, b):
                latent_heads, hs = BANKS[t][b]
                wide = (t + 1) * P
                act.wait_ge(shift_ready, bank_no(l, t, b) + 1)
                for j, hd in enumerate(hs):
                    col = hd if latent_heads else MH + hd
                    last = act.activation(probs[:, b % 2, j * wide:(j + 1) * wide],
                                          A[t][:, b % 2, j * wide:(j + 1) * wide], ACT.Exp,
                                          bias=shift[:, b % 2, j:j + 1],
                                          scale=MLA_SCALE if latent_heads else SWA_SCALE,
                                          accum_out=den[:, t, col:col + 1])
                if not latent_heads:
                    last = act.activation(sink_e[:, t, hs[0]:hs[-1] + 1], sink_gap[:, t, hs[0]:hs[-1] + 1],
                                          ACT.Exp)
                last.then_inc(probs_ready, 1)

            def probs_copy(l, t, b):
                w = len(BANKS[t][b][1]) * (t + 1) * P
                act.wait_ge(pt_psum, bank_no(l, t, b) + 1)
                act.activation(probs_t[:, b % 2, 0:w], UV[t][:, 0, 0:w], ACT.Copy).then_inc(pt_ready, 1)

            norm_squares(0, 0, 0)
            act.dma_start(x[:, 1, :], x_in[P:2 * P, :]).then_inc(x_loaded[1], 16)
            for b in range(2):
                split(0, -1, part=[b])
                norm_hi(0, 0, 0, [b])
            with act.Fori(0, DEPTH) as l:
                ffn(l, 0)
                silu_block, ht_high = ffn_group(l, 0, NG - 1)
                silu_block(0)
                ht_high(0)
                silu_block(1)
                split(l, MIX_AT + 1)
                ht_high(1)
                norm_squares(l, 1, 0)
                split(l, MIX_AT + 2)
                norm_hi(l, 1, 0)
                split(l, MIX_AT + 3)
                norm_squares(l, 1, 1)
                split(l, MIX_AT + 4)
                norm_hi(l, 1, 1)
                split(l, MIX_AT + 5)
                act.wait_ge(small_loaded, l * 32 + 32)
                latent_and_window(l, 0)
                latent_high(l, 0)
                mla_parts(l, 0)
                act.activation(sink_gap[:, 0, 0:1], consts[:, 0, 0:1], ACT.Exp)
                latent_and_window(l, 1)
                qk_copies(l, 0)
                swa_k_copy(l, 0)
                latent_high(l, 1)
                softmax(l, 0, 0)
                softmax(l, 0, 1)
                probs_copy(l, 0, 0)
                mla_parts(l, 1)
                probs_copy(l, 0, 1)
                softmax(l, 0, 2)
                probs_copy(l, 0, 2)
                softmax(l, 0, 3)
                qk_copies(l, 1)
                probs_copy(l, 0, 3)
                swa_k_copy(l, 1)
                norm_squares(l, 2, 0)
                split(l, MIX_AT + 6, part=[0])
                softmax(l, 1, 0)
                probs_copy(l, 1, 0)
                softmax(l, 1, 1)
                norm_hi(l, 2, 0)
                split(l, MIX_AT + 6, part=[1])
                probs_copy(l, 1, 1)
                softmax(l, 1, 2)
                split(l, MIX_AT + 7)
                probs_copy(l, 1, 2)
                softmax(l, 1, 3)
                attn_squares(l, 1, 0)
                probs_copy(l, 1, 3)
                softmax(l, 1, 4)
                split(l, MIX_AT + 8, part=[0])
                probs_copy(l, 1, 4)
                softmax(l, 1, 5)
                split(l, MIX_AT + 8, part=[1])
                probs_copy(l, 1, 5)
                split(l, MIX_AT + 9)
                attn_squares(l, 1, 1)
                norm_hi(l, 2, 1)
                norm_squares(l, 3, 0)
                split(l, FFN_AT[1])
                norm_hi(l, 3, 0)
                ffn(l, 1)
                silu_block, ht_high = ffn_group(l, 1, NG - 1)
                silu_block(0)
                ht_high(0)
                silu_block(1)
                ht_high(1)
                norm_squares(l, 4, 0)
                norm_hi(l, 4, 0)

        @block.vector
        def _(dve):
            def split(l, unit, i=0, di=0, part=range(2)):
                for half in part:
                    n = half_no(unit, half)
                    dve.wait_ge(hi_done, l * (2 * LU) + i * (2 * di) + (n + 1))
                    dve.tensor_tensor(wlo_half(unit, half), raw[:, n % RAW, :],
                                      whi_half(unit, half).bitcast(F32), ALU.subtract).then_inc(split_done, 1)

            def add_to_x(l, s, t):
                dve.wait_ge(sum_ready, l * 6 + (2 * s + t + 1))
                dve.scalar_tensor_tensor(x[:, t, :], A[t][:].rearrange("p a b -> p (a b)"),
                                         1.0 if s == 1 else 0.5, x[:, t, :], ALU.mult, ALU.add
                                         ).then_inc(x_ready, 1)

            def norm_apply(l, k, t):
                n = 2 * k + t
                if t == 0:
                    dve.wait_ge(gain_loaded[k % 2], l * 32 + 16 * (k // 2 + 1))
                dve.wait_ge(rstd_ready, l * 8 + (n + 1))
                if n:
                    dve.wait_ge(xt_ready, l * 16 + 2 * n)
                for b in range(2):
                    w = slice(b * 512, (b + 1) * 512)
                    src, c = (attn[:, w], b) if k == 2 else (x[:, t, w], 0)
                    dve.scalar_tensor_tensor(xn[:, w], src, rs_x[:, t, c:c + 1], gain[:, k % 2, w], ALU.mult,
                                             ALU.mult).then_inc(xn_ready, 1)

            def norm_lo(l, k, t, banks=range(2)):
                for b in banks:
                    dve.wait_ge(act_hi_done, l * 16 + (4 * k + 2 * t + b + 1))
                    dve.tensor_tensor(act_lo[:, t, 4 * b:4 * b + 4, :], heads(UV[t][:, b, :], 4),
                                      act_hi[:, t, 4 * b:4 * b + 4, :].bitcast(F32), ALU.subtract
                                      ).then_inc(act_ready, 1)

            def ffn_group(l, f, g, i=0):
                n = l * (4 * NG) + i * 2 + (2 * (NG * f + g) + 1)

                def gate_times_up(t):
                    dve.wait_ge(silu_done, n + t)
                    dve.tensor_tensor(h[:, t, :], silu[:, t, :], UV[t][:, 0, GC:2 * GC], ALU.mult
                                      ).then_inc(h_ready, 1)

                def ht_low(t):
                    dve.wait_ge(ht_hi_done, n + t)
                    at = ht_at(g, t)
                    dve.tensor_tensor(ht_lo[:, at], heads(UV[t][:, 1, 0:GC], 2), ht_hi[:, at].bitcast(F32),
                                      ALU.subtract).then_inc(ht_ready, 1)

                def transposed_and_splits():
                    ht_low(0)
                    if g + 2 < NG:
                        split(l, FFN_AT[f] + up_unit(g + 2), i, 3)
                        split(l, FFN_AT[f] + up_unit(g + 2) + 1, i, 3)
                    if g == 0:
                        ht_low(1)
                    split(l, FFN_AT[f] + down_unit(g + 1), i, 3)
                    if g + 2 == NG and f == 0:
                        split(l, MIX_AT)
                    elif g + 2 == NG:
                        split(l, NEXT_UNIT)
                    if g:
                        ht_low(1)

                if g == NG - 1:
                    return gate_times_up, ht_low
                if g == 0:
                    return gate_times_up, transposed_and_splits
                gate_times_up(0)
                gate_times_up(1)
                transposed_and_splits()

            def ffn(l, f):
                k = 3 * f
                if f == 1:
                    add_to_x(l, 1, 1)
                split(l, FFN_AT[f] + 1)
                norm_apply(l, k, 1)
                split(l, FFN_AT[f] + 2, part=[0])
                norm_lo(l, k, 1)
                gate_times_up, after = ffn_group(l, f, 0)
                gate_times_up(0)
                split(l, FFN_AT[f] + 2, part=[1])
                split(l, FFN_AT[f] + 3)
                gate_times_up(1)
                split(l, FFN_AT[f] + down_unit(0))
                after()
                with dve.Fori(0, NG - 3, 2) as i:
                    ffn_group(l, f, 1, i)
                    ffn_group(l, f, 2, i)
                ffn_group(l, f, NG - 2)

            def rotate(src, first, n, t, ready):
                dst = heads(qkn[:, first:first + n // 2, :].rearrange("p a b -> p (a b)"), n)
                src, tmp = heads(src, n), heads(rot_tmp[:, 0:n * ROPE], n)
                hf = ROPE // 2
                dve.tensor_tensor(dst, src, over_heads(cs[:, t, 0, :], n), ALU.mult)
                dve.tensor_tensor(tmp[:, :, 0:hf], src[:, :, hf:ROPE], over_heads(cs[:, t, 1, 0:hf], n), ALU.mult)
                dve.tensor_tensor(tmp[:, :, hf:ROPE], src[:, :, 0:hf], over_heads(cs[:, t, 1, hf:ROPE], n),
                                  ALU.mult)
                dve.drain()
                last = dve.tensor_tensor(dst, dst, tmp, ALU.add)
                if ready:
                    last.then_inc(qkn_ready, 1)

            def latent_norm(l, t):
                dve.wait_ge(latent_rstd, l * TB + (t + 1))
                dve.wait_ge(xt_ready, l * 16 + 8)
                dve.scalar_tensor_tensor(xn[:, 0:QR], A[t][:, 0, 0:QR], rs_c[:, t, 0:1],
                                         sgain[:, SG_QA:SG_QA + QR], ALU.mult, ALU.mult)
                dve.scalar_tensor_tensor(xn[:, QR:QR + KVR], A[t][:, 0, QR:QR + KVR], rs_c[:, t, 1:2],
                                         sgain[:, SG_KVA:SG_KVA + KVR], ALU.mult, ALU.mult
                                         ).then_inc(latent_ready, 1)

            def window_sums(l, t):
                dve.wait_ge(swa_copied, l * TB + (t + 1))
                flat = work[:].rearrange("p a b -> p (a b)")
                dve.reduce_sum(ss_s[:, t, :], heads(flat[:, 0:640], 10), axis=AX_X).then_inc(swa_ss, 1)

            def window_norm(l, t):
                dve.wait_ge(swa_rstd, l * TB + (t + 1))
                dve.tensor_tensor(heads(rot_in, 10), heads(swa_raw, 10), spread(rs_s[:, t, :], SD), ALU.mult
                                  ).then_inc(swa_used, 1)
                dve.drain()
                q, k = heads(rot_in[:, 0:512], SH), heads(rot_in[:, 512:640], SKV)
                dve.tensor_tensor(q, q, over_heads(sgain[:, SG_SQ:SG_SQ + SD], SH), ALU.mult)
                dve.tensor_tensor(k, k, over_heads(sgain[:, SG_SK:SG_SK + SD], SKV), ALU.mult)
                dve.drain()
                if t == 1:
                    dve.wait_ge(qk_psum, l * (5 * TB) + 5)
                rotate(rot_in, CSQ, 10, t, False)

            def latent_lo(l, t):
                dve.wait_ge(latent_hi_done, l * TB + (t + 1))
                dve.tensor_tensor(act_lo[:, t, 0:3, :], heads(UV[t][:, 1, 0:384], 3),
                                  act_hi[:, t, 0:3, :].bitcast(F32), ALU.subtract).then_inc(latent_act, 1)

            def mla_sums(l, t):
                dve.drain()
                dve.wait_ge(mla_done, l * TB + (t + 1))
                dve.tensor_copy(rot_in[:, 0:256], UV[t][:, 1, 0:256])
                if t == 0:
                    dve.tensor_copy(v_mla[:, t, :], A[t][:, 1, :])
                dve.drain()
                dve.scalar_tensor_tensor(rot_tmp[:, 0:256], rot_in[:, 0:256], 1.0 / MLA_QK, rot_in[:, 0:256],
                                         ALU.mult, ALU.mult)
                dve.drain()
                dve.reduce_sum(ss_part[:, t, 8:12], heads(rot_tmp[:, 0:256], MH), axis=AX_X)
                dve.tensor_tensor(kpe_g[:], kpe[:, t, :], sgain[:, SG_MK:SG_MK + ROPE], ALU.mult)
                dve.drain()
                dve.wait_ge(mla_squares, l * TB + (t + 1))
                dve.tensor_tensor(ss_m[:, t, 0:4], ss_part[:, t, 0:4], ss_part[:, t, 8:12], ALU.add)
                dve.tensor_scalar(ss_m[:, t, 4:8], ss_part[:, t, 4:8], ss_pe[:, t, :], None, ALU.add
                                  ).then_inc(mla_ss, 1)

            def mla_norm(l, t):
                dve.wait_ge(mla_rstd, l * TB + (t + 1))
                dve.tensor_tensor(qkn[:, CQN:CQN + 4, :], heads(UV[t][:, 0, :], MH), spread(rs_m[:, t, 0:4], NOPE),
                                  ALU.mult)
                dve.tensor_tensor(qkn[:, CKN:CKN + 4, :], heads(A[t][:, 0, :], MH), spread(rs_m[:, t, 4:8], NOPE),
                                  ALU.mult).then_inc(qkn_ready, 1)
                q, k = heads(rot_in[:, 0:256], MH), heads(rot_in[:, 256:512], MH)
                dve.tensor_tensor(q, q, spread(rs_m[:, t, 0:4], ROPE), ALU.mult)
                dve.tensor_tensor(k, over_heads(kpe_g[:], MH), spread(rs_m[:, t, 4:8], ROPE), ALU.mult)
                dve.drain()
                dve.tensor_tensor(q, q, over_heads(sgain[:, SG_MQ:SG_MQ + ROPE], MH), ALU.mult)
                dve.drain()
                rotate(rot_in[:, 0:512], CQR, 8, t, True)

            def qk_copies(l, t):
                dve.wait_ge(qk_psum, l * (5 * TB) + 5 * t + 4)
                dve.tensor_copy(qt[:, t, 4:6, :], heads(A[t][:, 1, 0:256], 2))
                dve.tensor_copy(kt[:, 0:2, t, :], heads(A[t][:, 1, 256:512], 2)).then_inc(qk_dve, 1)

            def maxima(l, t, b):
                latent_heads, hs = BANKS[t][b]
                n, c = bank_no(l, t, b), len(hs)
                dve.wait_ge(scores_done, n + 1)
                dve.reduce_max(maxi[:, b % 2, 0:c], heads(A[t][:, b % 2, 0:c * (t + 1) * P], c), axis=AX_X)
                dve.drain()
                if latent_heads:
                    dve.tensor_scalar(shift[:, b % 2, 0:c], maxi[:, b % 2, 0:c], -MLA_SCALE, None, ALU.mult
                                      ).then_inc(shift_ready, 1)
                    return
                sink = sgain[:, SG_SINK + hs[0]:SG_SINK + hs[0] + c]
                dve.scalar_tensor_tensor(top[:, b % 2, 0:c], maxi[:, b % 2, 0:c], SWA_SCALE, sink, ALU.mult,
                                         ALU.max)
                dve.drain()
                dve.tensor_tensor(sink_gap[:, t, hs[0]:hs[0] + c], sink, top[:, b % 2, 0:c], ALU.subtract)
                dve.tensor_scalar(shift[:, b % 2, 0:c], top[:, b % 2, 0:c], -1.0, None, ALU.mult
                                  ).then_inc(shift_ready, 1)

            def latent_result(l, t):
                dve.wait_ge(pv_done, bank_no(l, t, 1) + 1)
                dve.reciprocal(rden[:, t, 0:MH], den[:, t, 0:MH])
                dve.drain()
                dve.tensor_tensor(heads(attn[:, 0:512], MH), heads(UV[t][:, 1, :], MH),
                                  spread(rden[:, t, 0:MH], MV), ALU.mult).then_inc(attn_ready, 1)

            def window_result(l, t):
                dve.wait_ge(pv_done, bank_no(l, t, len(BANKS[t]) - 1) + 1)
                dve.tensor_tensor(rden[:, t, MH:], den[:, t, MH:], sink_e[:, t, :], ALU.add)
                dve.drain()
                dve.reciprocal(rden[:, t, MH:], rden[:, t, MH:])
                dve.drain()
                dve.tensor_tensor(heads(attn[:, 512:], SH), heads(UV[t][:, 1, :], SH),
                                  spread(rden[:, t, MH:], SD), ALU.mult).then_inc(attn_ready, 1)

            dve.memset(top[:], 0.0).then_inc(split_done, RAW)
            dve.wait_ge(x_loaded[0], 16)
            dve.memset(maxi[:], 0.0).then_inc(x_ready, 1)
            norm_apply(0, 0, 0)
            for b in range(2):
                split(0, -1, part=[b])
                norm_lo(0, 0, 0, [b])
            dve.wait_ge(x_loaded[1], 16)
            dve.memset(shift[:], 0.0).then_inc(x_ready, 1)
            with dve.Fori(0, DEPTH) as l:
                ffn(l, 0)
                gate_times_up, ht_low = ffn_group(l, 0, NG - 1)
                gate_times_up(0)
                ht_low(0)
                gate_times_up(1)
                add_to_x(l, 0, 0)
                ht_low(1)
                split(l, MIX_AT + 1)
                norm_apply(l, 1, 0)
                norm_lo(l, 1, 0)
                split(l, MIX_AT + 2)
                add_to_x(l, 0, 1)
                split(l, MIX_AT + 3)
                norm_apply(l, 1, 1)
                split(l, MIX_AT + 4, part=[0])
                norm_lo(l, 1, 1)
                split(l, MIX_AT + 4, part=[1])
                split(l, MIX_AT + 5)
                dve.wait_ge(small_loaded, l * 32 + 32)
                dve.wait_ge(rope_loaded, 16)
                latent_norm(l, 0)
                window_sums(l, 0)
                latent_lo(l, 0)
                window_norm(l, 0)
                mla_sums(l, 0)
                mla_norm(l, 0)
                latent_norm(l, 1)
                qk_copies(l, 0)
                window_sums(l, 1)
                latent_lo(l, 1)
                maxima(l, 0, 0)
                maxima(l, 0, 1)
                window_norm(l, 1)
                maxima(l, 0, 2)
                mla_sums(l, 1)
                latent_result(l, 0)
                maxima(l, 0, 3)
                mla_norm(l, 1)
                qk_copies(l, 1)
                window_result(l, 0)
                maxima(l, 1, 0)
                split(l, MIX_AT + 6, part=[0])
                maxima(l, 1, 1)
                norm_apply(l, 2, 0)
                maxima(l, 1, 2)
                norm_lo(l, 2, 0)
                split(l, MIX_AT + 6, part=[1])
                maxima(l, 1, 3)
                latent_result(l, 1)
                split(l, MIX_AT + 7)
                maxima(l, 1, 4)
                maxima(l, 1, 5)
                split(l, MIX_AT + 8)
                window_result(l, 1)
                split(l, MIX_AT + 9)
                norm_apply(l, 2, 1)
                norm_lo(l, 2, 1)
                add_to_x(l, 1, 0)
                norm_apply(l, 3, 0)
                split(l, FFN_AT[1])
                norm_lo(l, 3, 0)
                ffn(l, 1)
                gate_times_up, ht_low = ffn_group(l, 1, NG - 1)
                gate_times_up(0)
                ht_low(0)
                gate_times_up(1)
                add_to_x(l, 2, 0)
                ht_low(1)
                norm_apply(l, 4, 0)
                norm_lo(l, 4, 0)
                add_to_x(l, 2, 1)

        @block.tensor
        def _(pe):
            def halves_split(l, n, i=0):
                pe.wait_ge(split_done, l * (2 * LU) + i * 6 + (RAW + 2 + n + 1))

            def product(dst, hi, lo, w_hi, w_lo, start, stop):
                pe.matmul(dst, hi, w_hi, start=start, stop=False, skip_group_check=True)
                pe.matmul(dst, hi, w_lo, start=False, stop=False, skip_group_check=True)
                return pe.matmul(dst, lo, w_hi, start=False, stop=stop, skip_group_check=True)

            def transpose_norm(l, k, t):
                for c in range(KD):
                    if c % 4 == 0:
                        pe.wait_ge(xn_ready, l * 16 + (4 * k + 2 * t + c // 4 + 1))
                    last = pe.transpose(UV[t][:, c // 4, (c % 4) * P:(c % 4 + 1) * P], xn[:, c * P:(c + 1) * P],
                                        ident[:])
                    if c % 4 == 3:
                        last.then_inc(xt_ready, 1)
                    elif c == 0 and t == 1 and k != 2:
                        last.then_inc(unit_freed, 1)

            def activations(l, k, t, c):
                if c % 4 == 0:
                    pe.wait_ge(act_ready, l * 16 + (4 * k + 2 * t + c // 4 + 1))

            def up(l, f, g, t, chunks, i=0):
                if g and chunks[0] == 0:
                    pe.wait_ge(h_ready, l * (4 * NG) + i * 2 + (2 * (NG * f + g - 1) + t + 1))
                unit = FFN_AT[f] + up_unit(g)
                for k in chunks:
                    if g == 0:
                        activations(l, 3 * f, t, k)
                    if t == 0 and k % 2 == 0:
                        halves_split(l, 2 * unit + k // 2, i)
                    w = slice((k % 2) * 512, (k % 2 + 1) * 512)
                    u, hf = unit + k // 4, k // 2 % 2
                    last = product(UV[t][:, 0, :], act_hi[:, t, k, :], act_lo[:, t, k, :],
                                   whi_half(u, hf)[:, w], wlo_half(u, hf)[:, w], k == 0, k == KD - 1)
                if chunks[-1] == KD - 1:
                    last.then_inc(up_done, 1)
                return last

            def transpose_h(l, f, g, t, i=0):
                n = l * (4 * NG) + i * 2 + (2 * (NG * f + g) + t + 1)
                pe.wait_ge(h_ready, n)
                for c in range(2):
                    last = pe.transpose(UV[t][:, 1, c * P:(c + 1) * P], h[:, t, c * P:(c + 1) * P], ident[:])
                last.then_inc(ht_psum, 1)

            def down(l, f, g, t, c, i=0):
                unit, at = FFN_AT[f] + down_unit(g), ht_at(g, t)
                if c == 0:
                    pe.wait_ge(ht_ready, l * (4 * NG) + i * 2 + (2 * (NG * f + g) + t + 1))
                if t == 0:
                    halves_split(l, 2 * unit + c, i)
                for n in range(2):
                    w = slice(n * 512, (n + 1) * 512)
                    last = product(A[t][:, n, :], ht_hi[:, at, c, :], ht_lo[:, at, c, :],
                                   whi_half(unit, c)[:, w], wlo_half(unit, c)[:, w],
                                   g == 0 and c == 0, g == NG - 1 and c == 1)
                return last

            def ffn_step(l, f, g, i=0):
                for t in range(TB):
                    last = up(l, f, g, t, range(0, 4), i)
                    if g == 1 and t == 0:
                        last.then_inc(unit_freed, 2)
                    transpose_h(l, f, g - 1, t, i)
                    up(l, f, g, t, range(4, KD), i)
                    up_freed = down(l, f, g - 1, t, 0, i)
                    down_freed = down(l, f, g - 1, t, 1, i)
                up_freed.then_inc(unit_freed, 2)
                down_freed.then_inc(unit_freed, 1)

            def ffn(l, f):
                up(l, f, 0, 0, range(0, 6))
                transpose_norm(l, 3 * f, 1)
                up(l, f, 0, 0, range(6, KD))
                up(l, f, 0, 1, range(KD))
                ffn_step(l, f, 1)
                with pe.Fori(0, NG - 3, 2) as i:
                    ffn_step(l, f, 2, i)
                    ffn_step(l, f, 3, i)
                g = NG - 1
                up(l, f, g, 0, range(0, 4))
                transpose_h(l, f, g - 1, 0)
                up(l, f, g, 0, range(4, KD))
                down(l, f, g - 1, 0, 0)
                down(l, f, g - 1, 0, 1)
                up(l, f, g, 1, range(0, 4))
                transpose_h(l, f, g - 1, 1)
                up(l, f, g, 1, range(4, 6))
                transpose_h(l, f, g, 0)
                up(l, f, g, 1, range(6, KD))
                down(l, f, g, 0, 0).then_inc(unit_freed, 2)
                down(l, f, g, 0, 1).then_inc(sum_ready, 1)
                transpose_h(l, f, g, 1)
                down(l, f, g - 1, 1, 0)
                down(l, f, g - 1, 1, 1).then_inc(unit_freed, 1)
                down(l, f, g, 1, 0)
                transpose_norm(l, 1 if f == 0 else 4, 0)
                down(l, f, g, 1, 1).then_inc(sum_ready, 1)

            def input_main(l, t, chunks):
                for k in chunks:
                    u, hf = MIX_AT + k // 2, k % 2
                    activations(l, 1, t, k)
                    if t == 0:
                        halves_split(l, 2 * u + hf)
                    for n in range(2):
                        w = slice(n * 512, (n + 1) * 512)
                        last = product(A[t][:, n, :], act_hi[:, t, k, :], act_lo[:, t, k, :],
                                       whi_half(u, hf)[:, w], wlo_half(u, hf)[:, w], k == 0, k == KD - 1)
                if chunks[-1] == KD - 1:
                    last.then_inc(main_done, 1)

            def input_tail(l, t):
                for k in range(KD):
                    u, hf = MIX_AT + 4, k // 4
                    if t == 0 and k % 4 == 0:
                        halves_split(l, 2 * u + hf)
                    w = slice((k % 4) * 192, (k % 4 + 1) * 192)
                    last = product(UV[t][:, 0, 0:192], act_hi[:, t, k, :], act_lo[:, t, k, :],
                                   whi_half(u, hf)[:, w], wlo_half(u, hf)[:, w], k == 0, k == KD - 1)
                    if t == 1 and k == 0:
                        last.then_inc(unit_freed, 4)
                return last.then_inc(proj_done, 1)

            def transpose_latent(l, t):
                pe.wait_ge(latent_ready, l * TB + (t + 1))
                for c in range(3):
                    last = pe.transpose(UV[t][:, 1, c * P:(c + 1) * P], xn[:, c * P:(c + 1) * P], ident[:])
                last.then_inc(latent_psum, 1)

            def latent_products(l, t):
                pe.wait_ge(latent_act, l * TB + (t + 1))
                u = MIX_AT + 5
                if t == 0:
                    halves_split(l, 2 * u + 1)
                for n in range(2):
                    w = slice(n * 512, (n + 1) * 512)
                    product(A[t][:, n, :], act_hi[:, t, 2, :], act_lo[:, t, 2, :],
                            whi_half(u, 1)[:, w], wlo_half(u, 1)[:, w], True, True)
                for k in range(2):
                    w = slice(k * 512, (k + 1) * 512)
                    product(UV[t][:, 0, :], act_hi[:, t, k, :], act_lo[:, t, k, :],
                            whi_half(u, 0)[:, w], wlo_half(u, 0)[:, w], k == 0, k == 1)
                for k in range(2):
                    w = slice(768, 1024)
                    last = product(UV[t][:, 1, 0:256], act_hi[:, t, k, :], act_lo[:, t, k, :],
                                   whi_half(u - 1, k)[:, w], wlo_half(u - 1, k)[:, w], k == 0, k == 1)
                return last.then_inc(mla_done, 1)

            def transpose_qk(l, t, first, past):
                banks = [(A[t][:, 0, :], CQN), (UV[t][:, 0, :], CKN), (UV[t][:, 1, :], CSQ), (A[t][:, 1, :], CQR),
                         (A[t][:, 0, :], CSK)]
                for b in range(first, past):
                    if b == 0:
                        pe.wait_ge(qkn_ready, l * (2 * TB) + (2 * t + 1))
                    elif b == 3:
                        pe.wait_ge(qkn_ready, l * (2 * TB) + (2 * t + 2))
                    elif b == 4:
                        pe.wait_ge(qk_act, l * (2 * TB) + (2 * t + 1))
                    bank, at = banks[b]
                    for c in range(4 if b < 4 else 1):
                        last = pe.transpose(bank[:, c * P:(c + 1) * P], qkn[:, at + c, :], ident[:])
                    last.then_inc(qk_psum, 1)

            def scores(l, t, b):
                latent_heads, hs = BANKS[t][b]
                n, wide = bank_no(l, t, b), (t + 1) * P
                if b >= 2:
                    pe.wait_ge(probs_ready, n - 1)
                for j, hd in enumerate(hs):
                    dst = A[t][:, b % 2, j * wide:(j + 1) * wide]
                    if latent_heads:
                        r = ROPE * (hd % 2)
                        pe.matmul(dst, qt[:, t, hd, :], kt[:, 2 + hd, 0:t + 1, :], start=True, stop=False,
                                  skip_group_check=True)
                        pe.matmul(dst, qt[r:r + ROPE, t, 4 + hd // 2, :], kt[r:r + ROPE, hd // 2, 0:t + 1, :],
                                  start=False, stop=False, skip_group_check=True)
                        last = pe.matmul(dst[:, t * P:wide], ident_b[:], masks[:, 1, :], start=False, stop=True,
                                         skip_group_check=True)
                    else:
                        r = SD * (hd // 4)
                        pe.matmul(dst, qt[r:r + SD, t, 6 + hd % 4, :], kt[r:r + SD, 6, 0:t + 1, :], start=True,
                                  stop=False, skip_group_check=True)
                        last = pe.matmul(dst, ident_b[:], masks[:, 1 - t:2, :], start=False, stop=True,
                                         skip_group_check=True)
                    first = last if j == 0 else first
                last.then_inc(scores_done, 1)
                return first

            def transpose_probs(l, t, b):
                pe.wait_ge(probs_ready, bank_no(l, t, b) + 1)
                if b:
                    pe.wait_ge(pt_ready, bank_no(l, t, b))
                for c in range(len(BANKS[t][b][1]) * (t + 1)):
                    last = pe.transpose(UV[t][:, 0, c * P:(c + 1) * P], probs[:, b % 2, c * P:(c + 1) * P], ident[:])
                last.then_inc(pt_psum, 1)

            def values(l, t, b):
                latent_heads, hs = BANKS[t][b]
                n = bank_no(l, t, b)
                pe.wait_ge(pt_ready, n + 1)
                if not latent_heads and hs[0] == 0:
                    pe.wait_ge(attn_ready, l * 4 + (2 * t + 1))
                for j, hd in enumerate(hs):
                    for c in range(t + 1):
                        if latent_heads:
                            dst, v = UV[t][:, 1, hd * MV:(hd + 1) * MV], v_mla[:, c, hd * MV:(hd + 1) * MV]
                        else:
                            kv = hd // (SH // SKV)
                            dst, v = UV[t][:, 1, hd * SD:(hd + 1) * SD], v_swa[:, c, kv * SD:(kv + 1) * SD]
                        last = pe.matmul(dst, probs_t[:, b % 2, (j * (t + 1) + c) * P:(j * (t + 1) + c + 1) * P], v,
                                         start=c == 0, stop=c == t, skip_group_check=True)
                last.then_inc(pv_done, 1)

            def output_chunk(l, t, k):
                u, hf = MIX_AT + 6 + k // 2, k % 2
                activations(l, 2, t, k)
                if t == 0:
                    halves_split(l, 2 * u + hf)
                for n in range(2):
                    w = slice(n * 512, (n + 1) * 512)
                    last = product(A[t][:, n, :], act_hi[:, t, k, :], act_lo[:, t, k, :],
                                   whi_half(u, hf)[:, w], wlo_half(u, hf)[:, w], k == 0, k == KD - 1)
                if k == KD - 1:
                    last.then_inc(sum_ready, 1)
                elif k % 2 and t == 1:
                    last.then_inc(unit_freed, 1)

            pe.wait_ge(const_ready, 1)
            transpose_norm(0, 0, 0)
            with pe.Fori(0, DEPTH) as l:
                ffn(l, 0)
                input_main(l, 0, range(0, 6))
                transpose_norm(l, 1, 1)
                input_main(l, 0, range(6, KD))
                input_tail(l, 0)
                input_main(l, 1, range(0, 2))
                transpose_latent(l, 0)
                input_main(l, 1, range(2, 4))
                latent_products(l, 0)
                input_main(l, 1, range(4, KD))
                input_tail(l, 1)
                transpose_qk(l, 0, 0, 5)
                transpose_latent(l, 1)
                pe.wait_ge(qk_act, l * (2 * TB) + 2)
                pe.wait_ge(qk_dve, l * TB + 1)
                scores(l, 0, 0)
                scores(l, 0, 1)
                latent_products(l, 1)
                transpose_probs(l, 0, 0)
                scores(l, 0, 2).then_inc(unit_freed, 2)
                values(l, 0, 0)
                transpose_probs(l, 0, 1)
                scores(l, 0, 3)
                values(l, 0, 1)
                transpose_probs(l, 0, 2)
                values(l, 0, 2)
                transpose_qk(l, 1, 0, 3)
                transpose_probs(l, 0, 3)
                transpose_qk(l, 1, 3, 5)
                values(l, 0, 3)
                pe.wait_ge(qk_act, l * (2 * TB) + 4)
                pe.wait_ge(qk_dve, l * TB + 2)
                scores(l, 1, 0)
                scores(l, 1, 1)
                k = 0
                for b in range(len(BANKS[1])):
                    transpose_probs(l, 1, b)
                    if b + 2 < len(BANKS[1]):
                        scores(l, 1, b + 2)
                    if b == 0:
                        transpose_norm(l, 2, 0)
                    elif b != 3:
                        output_chunk(l, 0, k)
                        k += 1
                    values(l, 1, b)
                for k in range(4, KD - 1):
                    output_chunk(l, 0, k)
                transpose_norm(l, 2, 1)
                output_chunk(l, 0, KD - 1)
                for k in range(KD):
                    output_chunk(l, 1, k)
                    if k == 3:
                        transpose_norm(l, 3, 0)
                ffn(l, 1)


def kernel(**inputs):
    import numpy as np
    import concourse.bacc as bacc
    from concourse.bass_utils import run_bass_kernel_spmd as run

    a = {n: np.ascontiguousarray(v) for n, v in inputs.items()}

    def halves(l):
        out = []

        def up(f, g):
            w = [a[f"ffn{f + 1}_w_{n}"][l][:, g * GC:(g + 1) * GC].reshape(KD // 2, 2, P, GC)
                 for n in ("gate", "up")]
            out.extend(np.stack(w, 3).transpose(0, 2, 1, 3, 4).reshape(KD // 2, P, HC))

        def down(f, g):
            out.extend(a[f"ffn{f + 1}_w_down"][l][g * GC:(g + 1) * GC].reshape(2, P, HC))

        def ffn(f):
            up(f, 0)
            up(f, 1)
            for g in range(NG):
                down(f, g)
                if g + 2 < NG:
                    up(f, g + 2)

        ffn(0)
        w = a["w_in"][l]
        at = np.cumsum([0, QR, KVR, ROPE, SH * SD, SKV * SD, SKV * SD])
        cq, ckv, kpe, qs, ks, vs = (w[:, at[j]:at[j + 1]] for j in range(6))
        qs = qs.reshape(D, SKV, SH // SKV, SD).transpose(0, 2, 1, 3).reshape(D, SH * SD)
        out.extend(np.concatenate([cq, ckv, ks, qs], 1).reshape(KD, P, HC))
        tail = np.concatenate([vs, kpe], 1).reshape(2, 4, P, 192).transpose(0, 2, 1, 3).reshape(2, P, 768)
        qb = a["mla_w_q_b"][l].reshape(2, P, MH, MLA_QK)
        q_nope, q_rope = qb[..., :NOPE].reshape(2, P, 512), qb[..., NOPE:].reshape(2, P, 256)
        out.extend(np.concatenate([tail, q_rope], 2))
        out.append(q_nope.transpose(1, 0, 2).reshape(P, HC))
        out.append(a["mla_w_kv_b"][l].reshape(P, MH, 2, P).transpose(0, 2, 1, 3).reshape(P, HC))
        out.extend(a["w_o"][l].reshape(KD, P, HC))
        ffn(1)
        return out

    f32 = np.float32
    stream = np.stack([t for l in range(DEPTH) for t in halves(l)])
    norm_gains = np.stack([g for l in range(DEPTH) for g in (
        a["ffn1_norm"][l], a["mix_norm"][l], np.concatenate([a["mla_out_norm"][l], a["swa_out_norm"][l]]),
        a["ffn2_norm"][l])] + [a["ffn1_norm"][0]])
    small = np.concatenate([a["mla_q_a_norm"], a["mla_kv_a_norm"], a["swa_q_norm"], a["swa_k_norm"],
                            a["mla_q_norm"][:, NOPE:], a["mla_k_norm"][:, NOPE:], a["swa_sinks"]], 1)
    cols = np.ascontiguousarray(np.stack([a["mla_q_norm"][:, :NOPE], a["mla_k_norm"][:, :NOPE]], 2))
    inv = 1.0 / (f32(10000.0) ** (np.arange(0, ROPE, 2, dtype=f32) / f32(ROPE)))
    angle = np.arange(SEQ, dtype=f32)[:, None] * inv[None, :].astype(f32)
    c, s = np.cos(angle).astype(f32), np.sin(angle).astype(f32)
    rope = np.stack([np.concatenate([c, c], 1), np.concatenate([-s, s], 1)], 1).reshape(TB, P, 2, ROPE)

    arrays = {"x_in": a["x"].reshape(SEQ, D), "stream": stream, "norm_gains": norm_gains, "small_gains": small,
              "col_gains": cols, "rope": np.ascontiguousarray(rope)}
    nc = bacc.Bacc("TRN2", target_bir_lowering=False, num_devices=1)
    args = [nc.dram_tensor(n, v.shape, F32, kind="ExternalInput").ap() for n, v in arrays.items()]
    result = nc.dram_tensor("out", (SEQ, D), F32, kind="ExternalOutput").ap()
    hybrid_trunk(nc, *args, result)
    r = run(nc, [arrays], core_ids=[0])
    return r.results[0]["out"].reshape(1, SEQ, D)
```
